# Optimizing a Trainium2 kernel written in Bass

```python
import jax, jax.numpy as jnp
from jax import lax
import numpy as np
import math

D_MODEL = 1024
BATCH = 1
SEQ = 512
DEPTH = 1

CHUNK = 64
N_META = 16
Q_BLOCK = 128
EPS = 1e-6
ROPE_THETA = 10000.0
CONV_W = 256
CONV_K = 3
MLA_HEADS = 8
QK_NOPE = 64
QK_ROPE = 32
QK_HEAD = QK_NOPE + QK_ROPE
V_HEAD = 64
MLA_W = MLA_HEADS * V_HEAD
Q_RANK = 256
KV_RANK = 128
RET_HEADS = 4
RET_HEAD = 64
RET_W = RET_HEADS * RET_HEAD
D_MIX = CONV_W + MLA_W + RET_W
IN_SPLITS = (CONV_W, CONV_W, CONV_W, CONV_W, Q_RANK, KV_RANK, QK_ROPE, MLA_W, RET_W, RET_W, RET_W, RET_W)
D_IN = int(np.sum(IN_SPLITS))
IN_OFFSETS = tuple(int(o) for o in np.cumsum(IN_SPLITS)[:-1])


def rms_norm(x, w):
    xf = x.astype(jnp.float32)
    y = xf * lax.rsqrt(jnp.mean(xf * xf, axis=-1, keepdims=True) + EPS)
    return (y * w.astype(jnp.float32)).astype(x.dtype)

def rope_tables(n_pos, dim, dtype):
    inv = 1.0 / (ROPE_THETA ** (jnp.arange(0, dim, 2, dtype=jnp.float32) / dim))
    ang = jnp.arange(n_pos, dtype=jnp.float32)[:, None] * inv[None, :]
    return jnp.cos(ang).astype(dtype), jnp.sin(ang).astype(dtype)

def apply_rope(x, cos, sin):
    x1, x2 = jnp.split(x, 2, axis=-1)
    c = cos[:, None, :]
    s = sin[:, None, :]
    return jnp.concatenate([x1 * c - x2 * s, x1 * s + x2 * c], axis=-1)

def chunk_ids(n):
    pos = jnp.arange(n)
    return jnp.where(pos < N_META, 0, 1 + (pos - N_META) // CHUNK)

def short_conv_mixer(xin, b, c, z, conv_w, conv_b):
    L = xin.shape[1]
    u = jnp.pad(c * xin, ((0, 0), (CONV_K - 1, 0), (0, 0)))
    y = conv_b
    for j in range(CONV_K):
        y = y + u[:, j:j + L] * conv_w[j]
    return b * y * jax.nn.silu(z)

def mla_mixer(c_q, c_kv, k_rope, z, q_a_norm, w_uq, kv_a_norm, w_ukv, q_norm, k_norm, cos, sin):
    B, L, _ = c_q.shape
    q = (rms_norm(c_q, q_a_norm) @ w_uq).reshape(B, L, MLA_HEADS, QK_HEAD)
    kv = (rms_norm(c_kv, kv_a_norm) @ w_ukv).reshape(B, L, MLA_HEADS, QK_NOPE + V_HEAD)
    k_nope, v = kv[..., :QK_NOPE], kv[..., QK_NOPE:]
    k_r = jnp.broadcast_to(k_rope[:, :, None, :], (B, L, MLA_HEADS, QK_ROPE))
    k = jnp.concatenate([k_nope, k_r], axis=-1)
    q = rms_norm(q, q_norm)
    k = rms_norm(k, k_norm)
    q = jnp.concatenate([q[..., :QK_NOPE], apply_rope(q[..., QK_NOPE:], cos, sin)], axis=-1)
    k = jnp.concatenate([k[..., :QK_NOPE], apply_rope(k[..., QK_NOPE:], cos, sin)], axis=-1)
    Lp = -(-L // Q_BLOCK) * Q_BLOCK
    pad = ((0, 0), (0, Lp - L), (0, 0), (0, 0))
    q = jnp.pad(q, pad)
    k = jnp.pad(k, pad)
    v = jnp.pad(v, pad)
    cid = chunk_ids(Lp)
    n_blk = Lp // Q_BLOCK
    q_blocks = q.reshape(B, n_blk, Q_BLOCK, MLA_HEADS, QK_HEAD).transpose(1, 0, 2, 3, 4)
    cid_blocks = cid.reshape(n_blk, Q_BLOCK)
    scale = QK_HEAD ** -0.5
    neg = jnp.finfo(jnp.float32).min

    def attend(args):
        qb, qc = args
        s = jnp.einsum('bqhd,bkhd->bhqk', qb, k).astype(jnp.float32) * scale
        mask = cid[None, :] <= qc[:, None]
        s = jnp.where(mask[None, None], s, neg)
        p = jax.nn.softmax(s, axis=-1).astype(v.dtype)
        return jnp.einsum('bhqk,bkhd->bqhd', p, v)

    o = lax.map(attend, (q_blocks, cid_blocks))
    o = o.transpose(1, 0, 2, 3, 4).reshape(B, Lp, MLA_W)[:, :L]
    return o * jax.nn.silu(z)

def retention_mixer(q, k, v, z, ret_norm, cos, sin):
    B, L, _ = q.shape
    dt = q.dtype
    q = apply_rope(q.reshape(B, L, RET_HEADS, RET_HEAD), cos, sin)
    k = apply_rope(k.reshape(B, L, RET_HEADS, RET_HEAD), cos, sin) * (RET_HEAD ** -0.5)
    v = v.reshape(B, L, RET_HEADS, RET_HEAD)
    front = CHUNK - N_META
    back = (-(front + L)) % CHUNK
    pad = ((0, 0), (front, back), (0, 0), (0, 0))
    n_chk = (front + L + back) // CHUNK
    qc = jnp.pad(q, pad).reshape(B, n_chk, CHUNK, RET_HEADS, RET_HEAD)
    kc = jnp.pad(k, pad).reshape(B, n_chk, CHUNK, RET_HEADS, RET_HEAD)
    vc = jnp.pad(v, pad).reshape(B, n_chk, CHUNK, RET_HEADS, RET_HEAD)
    log_g = jnp.log1p(-jnp.exp2(-5.0 - jnp.arange(RET_HEADS, dtype=jnp.float32)))
    idx = jnp.arange(CHUNK, dtype=jnp.float32)
    intra_decay = jnp.exp(log_g[:, None, None] * jnp.abs(idx[:, None] - idx[None, :])).astype(dt)
    kv_decay = jnp.exp(log_g[:, None] * (CHUNK - 1.0 - idx)[None, :]).astype(dt)
    q_decay = jnp.exp(log_g[:, None] * (idx + 1.0)[None, :]).astype(dt)
    chunk_decay = jnp.exp(log_g * CHUNK).astype(dt)
    s = jnp.einsum('bnchd,bnmhd->bnhcm', qc, kc) * intra_decay
    o_intra = jnp.einsum('bnhcm,bnmhd->bnchd', s, vc)
    kv = jnp.einsum('bnmhd,hm,bnmhe->nbhde', kc, kv_decay, vc)

    def step(state, kv_n):
        return state * chunk_decay[None, :, None, None] + kv_n, state

    _, prev = lax.scan(step, jnp.zeros_like(kv[0]), kv)
    o_cross = jnp.einsum('bnchd,nbhde->bnche', qc, prev) * q_decay.T[None, None, :, :, None]
    o = (o_intra + o_cross).reshape(B, n_chk * CHUNK, RET_HEADS, RET_HEAD)[:, front:front + L]
    o = rms_norm(o, ret_norm).reshape(B, L, RET_W)
    return o * jax.nn.silu(z)

def first_inputs(seed: int = 0) -> dict:
    key = jax.random.key(seed)
    ks = jax.random.split(key, 16)
    f32 = jnp.float32

    def nrm(k, shape, scale):
        return jax.random.normal(k, shape, f32) * scale

    def gain(k, shape):
        return 1.0 + 0.05 * jax.random.normal(k, shape, f32)

    return {
        "x": jax.random.normal(ks[0], (BATCH, SEQ, D_MODEL), f32),
        "meta_tokens": nrm(ks[1], (N_META, D_MODEL), 1.0),
        "ln_w": gain(ks[2], (DEPTH, D_MODEL)),
        "w_in": nrm(ks[3], (DEPTH, D_MODEL, D_IN), D_MODEL ** -0.5),
        "w_out": nrm(ks[4], (DEPTH, D_MIX, D_MODEL), D_MIX ** -0.5),
        "conv_w": nrm(ks[5], (DEPTH, CONV_K, CONV_W), CONV_K ** -0.5),
        "conv_b": nrm(ks[6], (DEPTH, CONV_W), 0.02),
        "q_a_norm": gain(ks[7], (DEPTH, Q_RANK)),
        "w_uq": nrm(ks[8], (DEPTH, Q_RANK, MLA_HEADS * QK_HEAD), Q_RANK ** -0.5),
        "kv_a_norm": gain(ks[9], (DEPTH, KV_RANK)),
        "w_ukv": nrm(ks[10], (DEPTH, KV_RANK, MLA_HEADS * (QK_NOPE + V_HEAD)), KV_RANK ** -0.5),
        "q_norm": gain(ks[11], (DEPTH, QK_HEAD)),
        "k_norm": gain(ks[12], (DEPTH, QK_HEAD)),
        "ret_norm": gain(ks[13], (DEPTH, RET_HEAD)),
    }

def first_block(x, meta_tokens, ln_w, w_in, w_out, conv_w, conv_b, q_a_norm, w_uq, kv_a_norm, w_ukv,
              q_norm, k_norm, ret_norm):
    B = x.shape[0]
    meta = jnp.broadcast_to(meta_tokens[None].astype(x.dtype), (B, N_META, D_MODEL))
    h = jnp.concatenate([meta, x], axis=1)
    L = h.shape[1]
    cos_m, sin_m = rope_tables(L, QK_ROPE, h.dtype)
    cos_r, sin_r = rope_tables(L, RET_HEAD, h.dtype)
    for l in range(DEPTH):
        u = rms_norm(h, ln_w[l])
        (cx, cb, cc, cz, cq, ckv, krope, mz, rq, rk, rv, rz) = jnp.split(u @ w_in[l], IN_OFFSETS, axis=-1)
        y_conv = short_conv_mixer(cx, cb, cc, cz, conv_w[l], conv_b[l])
        y_mla = mla_mixer(cq, ckv, krope, mz, q_a_norm[l], w_uq[l], kv_a_norm[l], w_ukv[l],
                          q_norm[l], k_norm[l], cos_m, sin_m)
        y_ret = retention_mixer(rq, rk, rv, rz, ret_norm[l], cos_r, sin_r)
        y = jnp.concatenate([y_conv, y_mla, y_ret], axis=-1)
        h = h + y @ w_out[l]
    return h[:, N_META:]


MIX_WIDTH = D_MODEL
ATTN_WIDTH = MIX_WIDTH // 2
CONV_WIDTH = MIX_WIDTH - ATTN_WIDTH
HEAD_DIM = 64
N_HEADS = ATTN_WIDTH // HEAD_DIM
DILATED_PATTERNS = ((128, 1), (512, 4), (2048, 16))
CONV_KERNEL = 31
N_EXPERTS = 16
CAPACITY_FACTOR = 2
D_FF_EXPERT = 2816
NEG_INF = -1e30
IN_COLS = 3 * ATTN_WIDTH + 2 * CONV_WIDTH


def rms_norm_2(x, g):
    xf = x.astype(jnp.float32)
    y = xf * lax.rsqrt(jnp.mean(xf * xf, axis=-1, keepdims=True) + EPS)
    return (y * g.astype(jnp.float32)).astype(x.dtype)

def layer_norm(x, g, b):
    xf = x.astype(jnp.float32)
    mu = jnp.mean(xf, axis=-1, keepdims=True)
    xc = xf - mu
    y = xc * lax.rsqrt(jnp.mean(xc * xc, axis=-1, keepdims=True) + EPS)
    return (y * g.astype(jnp.float32) + b.astype(jnp.float32)).astype(x.dtype)

def rope(x, positions):
    half = x.shape[-1] // 2
    inv_freq = ROPE_THETA ** (-jnp.arange(half, dtype=jnp.float32) / half)
    ang = positions.astype(jnp.float32)[:, None] * inv_freq[None, :]
    cos, sin = jnp.cos(ang), jnp.sin(ang)
    xf = x.astype(jnp.float32)
    x1, x2 = xf[..., :half], xf[..., half:]
    out = jnp.concatenate([x1 * cos - x2 * sin, x2 * cos + x1 * sin], axis=-1)
    return out.astype(x.dtype)

def banded_attention(q, k, v, n):
    L, hd = q.shape[-2], q.shape[-1]
    lead = q.shape[:-2]
    nb = -(-L // n)
    Lp = nb * n
    lp = [(0, 0)] * len(lead)
    qb = jnp.pad(q, lp + [(0, Lp - L), (0, 0)]).reshape(*lead, nb, n, hd)

    def windows(t):
        tp = jnp.pad(t, lp + [(n, Lp - L + n), (0, 0)]).reshape(*lead, nb + 2, n, hd)
        return jnp.concatenate([tp[..., 0:nb, :, :], tp[..., 1:nb + 1, :, :],
                                tp[..., 2:nb + 2, :, :]], axis=-2)

    kw, vw = windows(k), windows(v)
    j = jnp.arange(nb)[:, None, None]
    qpos = j * n + jnp.arange(n)[None, :, None]
    kpos = j * n - n + jnp.arange(3 * n)[None, None, :]
    mask = (jnp.abs(qpos - kpos) <= n) & (kpos >= 0) & (kpos < L)
    s = jnp.einsum('...jqd,...jkd->...jqk', qb.astype(jnp.float32),
                   kw.astype(jnp.float32)) * (hd ** -0.5)
    s = jnp.where(mask, s, NEG_INF)
    m = jnp.max(s, axis=-1, keepdims=True)
    p = jnp.exp(s - m)
    l = jnp.sum(p, axis=-1, keepdims=True)
    o = jnp.einsum('...jqk,...jkd->...jqd', p, vw.astype(jnp.float32)) / l
    lse = (m + jnp.log(l))[..., 0]
    o = o.reshape(*lead, Lp, hd)[..., :L, :]
    lse = lse.reshape(*lead, Lp)[..., :L]
    return o, lse

def dilated_attention(q, k, v, window, dilation):
    B, H, S, hd = q.shape
    L = S // dilation

    def split(t):
        return t.reshape(B, H, L, dilation, hd).swapaxes(2, 3)

    o, lse = banded_attention(split(q), split(k), split(v), window // (2 * dilation))
    o = o.swapaxes(2, 3).reshape(B, H, S, hd)
    lse = lse.swapaxes(2, 3).reshape(B, H, S)
    return o, lse

def conformer_conv(a, b, dw_w, dw_b, ln_g, ln_b):
    u = a * jax.nn.sigmoid(b)
    C = u.shape[-1]
    pad = CONV_KERNEL // 2
    u = lax.conv_general_dilated(u, dw_w[:, None, :], window_strides=(1,),
                                 padding=[(pad, pad)],
                                 dimension_numbers=('NWC', 'WIO', 'NWC'),
                                 feature_group_count=C) + dw_b
    u = layer_norm(u, ln_g, ln_b)
    return jax.nn.silu(u)

def expert_choice_moe(h, w_router, w1, w3, w2):
    B, S, D = h.shape
    aff = jax.nn.softmax(jnp.einsum('bsd,de->bse', h, w_router).astype(jnp.float32), axis=-1)
    cap = CAPACITY_FACTOR * S // N_EXPERTS
    gate, idx = lax.top_k(aff.swapaxes(1, 2), cap)
    xe = jax.vmap(lambda hb, ib: hb[ib])(h, idx)

    def expert(args):
        xt, w1e, w3e, w2e = args
        return (jax.nn.silu(xt @ w1e) * (xt @ w3e)) @ w2e

    ye = lax.map(expert, (xe.swapaxes(0, 1), w1, w3, w2))
    ye = ye.swapaxes(0, 1) * gate[..., None].astype(ye.dtype)
    ye = ye.reshape(B, N_EXPERTS * cap, D)
    return jax.vmap(lambda y, i: jnp.zeros((S, D), y.dtype).at[i].add(y))(
        ye, idx.reshape(B, N_EXPERTS * cap))

def second_inputs(seed: int = 0) -> dict:
    key = jax.random.key(seed)
    ks = jax.random.split(key, 16)
    f32 = jnp.float32
    nrm = lambda k, shape, scale: jax.random.normal(k, shape, f32) * scale
    return {
        "x": jax.random.normal(ks[0], (BATCH, SEQ, D_MODEL), f32),
        "norm1_g": 1.0 + nrm(ks[1], (D_MODEL,), 0.02),
        "w_in": nrm(ks[2], (D_MODEL, IN_COLS), D_MODEL ** -0.5),
        "q_norm_g": 1.0 + nrm(ks[3], (HEAD_DIM,), 0.02),
        "k_norm_g": 1.0 + nrm(ks[4], (HEAD_DIM,), 0.02),
        "conv_dw_w": nrm(ks[5], (CONV_KERNEL, CONV_WIDTH), CONV_KERNEL ** -0.5),
        "conv_dw_b": nrm(ks[6], (CONV_WIDTH,), 0.01),
        "conv_ln_g": 1.0 + nrm(ks[7], (CONV_WIDTH,), 0.02),
        "conv_ln_b": nrm(ks[8], (CONV_WIDTH,), 0.01),
        "w_out": nrm(ks[9], (MIX_WIDTH, D_MODEL), MIX_WIDTH ** -0.5),
        "norm2_g": 1.0 + nrm(ks[10], (D_MODEL,), 0.02),
        "w_router": nrm(ks[11], (D_MODEL, N_EXPERTS), D_MODEL ** -0.5),
        "w1": nrm(ks[12], (N_EXPERTS, D_MODEL, D_FF_EXPERT), D_MODEL ** -0.5),
        "w3": nrm(ks[13], (N_EXPERTS, D_MODEL, D_FF_EXPERT), D_MODEL ** -0.5),
        "w2": nrm(ks[14], (N_EXPERTS, D_FF_EXPERT, D_MODEL), D_FF_EXPERT ** -0.5),
    }

def second_block(x, norm1_g, w_in, q_norm_g, k_norm_g, conv_dw_w, conv_dw_b,
              conv_ln_g, conv_ln_b, w_out, norm2_g, w_router, w1, w3, w2):
    B, S, D = x.shape
    positions = jnp.arange(S)
    for _ in range(DEPTH):
        h = rms_norm_2(x, norm1_g)
        z = jnp.einsum('bsd,dc->bsc', h, w_in)
        A = ATTN_WIDTH

        def heads(t):
            return t.reshape(B, S, N_HEADS, HEAD_DIM).transpose(0, 2, 1, 3)

        q = rope(rms_norm_2(heads(z[..., 0:A]), q_norm_g), positions)
        k = rope(rms_norm_2(heads(z[..., A:2 * A]), k_norm_g), positions)
        v = heads(z[..., 2 * A:3 * A])
        outs, lses = [], []
        for window, dilation in DILATED_PATTERNS:
            o_p, lse_p = dilated_attention(q, k, v, window, dilation)
            outs.append(o_p)
            lses.append(lse_p)
        w_mix = jax.nn.softmax(jnp.stack(lses), axis=0)
        attn = jnp.einsum('pbhs,pbhsd->bhsd', w_mix, jnp.stack(outs))
        attn = attn.transpose(0, 2, 1, 3).reshape(B, S, A).astype(x.dtype)

        c0 = 3 * A
        conv = conformer_conv(z[..., c0:c0 + CONV_WIDTH],
                              z[..., c0 + CONV_WIDTH:c0 + 2 * CONV_WIDTH],
                              conv_dw_w, conv_dw_b, conv_ln_g, conv_ln_b)
        mixed = jnp.concatenate([attn, conv.astype(x.dtype)], axis=-1)
        x = x + jnp.einsum('bsc,cd->bsd', mixed, w_out)

        x = x + expert_choice_moe(rms_norm_2(x, norm2_g), w_router, w1, w3, w2)
    return x


def setup_inputs(seed=0):
    out = dict(first_inputs(seed))
    for name, value in second_inputs(seed + 1).items():
        if name != "x":
            out[name + "_2"] = value
    return out


def reference(
    x, meta_tokens, ln_w, w_in, w_out, conv_w, conv_b, q_a_norm, w_uq, kv_a_norm, w_ukv, q_norm,
    k_norm, ret_norm, norm1_g_2, w_in_2, q_norm_g_2, k_norm_g_2, conv_dw_w_2, conv_dw_b_2,
    conv_ln_g_2, conv_ln_b_2, w_out_2, norm2_g_2, w_router_2, w1_2, w3_2, w2_2,
):
    x = first_block(
        x, meta_tokens, ln_w, w_in, w_out, conv_w, conv_b, q_a_norm, w_uq, kv_a_norm, w_ukv,
        q_norm, k_norm, ret_norm,
    )
    return second_block(
        x, norm1_g_2, w_in_2, q_norm_g_2, k_norm_g_2, conv_dw_w_2, conv_dw_b_2, conv_ln_g_2,
        conv_ln_b_2, w_out_2, norm2_g_2, w_router_2, w1_2, w3_2, w2_2,
    )


_drawn_inputs = setup_inputs


def setup_inputs(seed=0):
    import zlib

    import numpy as np

    out = dict(_drawn_inputs(seed))
    spreads = {}
    factors = {'conv_b': 5.803,
     'q_a_norm': 8.0,
     'kv_a_norm': 6.714,
     'q_norm': 8.0,
     'k_norm': 8.0,
     'ret_norm': 3.117,
     'norm1_g_2': 4.703,
     'q_norm_g_2': 8.0,
     'k_norm_g_2': 8.0,
     'conv_dw_b_2': 5.858,
     'conv_ln_g_2': 13.539,
     'conv_ln_b_2': 8.0,
     'norm2_g_2': 4.129}
    for name, (base, spread) in spreads.items():
        noise = np.random.default_rng([zlib.crc32(name.encode()), seed]).standard_normal(out[name].shape)
        drawn = base * np.exp(spread * noise) if base else spread * noise
        out[name] = __import__('jax').numpy.asarray(drawn.astype(out[name].dtype))
    for name, factor in factors.items():
        out[name] = (out[name] * factor).astype(out[name].dtype)
    return out
```

```python
from contextlib import ExitStack

import numpy as np

import concourse.bass as bass
from concourse import mybir

F32 = mybir.dt.float32
U32 = mybir.dt.uint32
ALU = mybir.AluOpType
ACT = mybir.ActivationFunctionType
AX = mybir.AxisListType

P = 128
D = 1024
KD = D // P
S = 512
NT = S // P
META = 16
LT = S + META
EPS = 1e-6
NEG = -1.0e30
QH, NOPE, ROPE, VH, MH = 96, 64, 32, 64, 8
RH, RD = 4, 64
C_CX, C_CB, C_CC, C_CZ, C_Q, C_KR, C_RQ, C_RV = 0, 256, 512, 768, 1024, 1408, 1952, 2464
H2, HD = 8, 64
TAPS, PAD = 31, 15
CW = S + 2 * PAD
E, CAP, FF = 16, 64, 2816
FH = FF // 2
FJ = FH // P
FCH = [(0, 512), (512, 512), (1024, 384)]

TOTAL = 53200
R13, R2 = 0, KD * FF
N2 = 11
WS = R2 + N2 * D
WSLOT = KD * 544
XOFF = WS + 2 * WSLOT
SMALL = XOFF + NT * D

PRM = {}


def _prm_layout():
    at = 0
    for name, n in (("lnw", 8), ("qan", 2), ("kvan", 1), ("qn", 1), ("kn", 1), ("cw", 6), ("cb", 2), ("n1g", 8),
                    ("dw", 4 * TAPS), ("dwb", 4), ("lng", 4), ("lnb", 4), ("n2g", 8),
                    ("qr", 32), ("qrs", 32), ("kr", 32), ("krs", 32), ("retn", 64),
                    ("q2", 64), ("q2s", 64), ("k2", 64), ("k2s", 64)):
        PRM[name] = (at, n)
        at += n
    return at


NPRM = _prm_layout()
TAB = {}


def _tab_layout():
    at = 0
    for name, n in (("mcc", 5 * 32), ("mss", 5 * 32), ("rcc", 5 * 64), ("rss", 5 * 64), ("bcc", 4 * 64), ("bss", 4 * 64),
                    ("dec", RH * LT), ("cm", 2 * S - P)):
        TAB[name] = (at, n)
        at += n
    return at


NTAB = _tab_layout()
GROUPS = [("w_in", [(C_Q, 384)]), ("w_in", [(C_KR, 544)]), ("w_in", [(C_RQ, 512)]), ("w_in", [(C_RV, 512)]),
          ("w_in", [(C_CC, 256), (C_CX, 256)]), ("w_in", [(C_CZ, 256), (C_CB, 256)]),
          ("w_out", [(0, 512)]), ("w_out", [(512, 512)]),
          ("w_in_2", [(2048, 256), (1536, 256)]), ("w_in_2", [(2304, 256), (1792, 256)]),
          ("w_in_2", [(0, 512)]), ("w_in_2", [(512, 512)]), ("w_in_2", [(1024, 512)]),
          ("w_out_2", [(0, 512)]), ("w_out_2", [(512, 512)])]


class Carve:

    def __init__(self, arena, at, end):
        self.arena, self.at, self.end = arena, at, end

    def __call__(self, n):
        a = self.at
        self.at += n
        assert self.at <= self.end, (self.at, self.end)
        return self.arena[:, a:a + n]


class Own:

    def __init__(self, eng, sem):
        self.eng, self.sem, self.n = eng, sem, 0

    def __call__(self, ins):
        ins.then_inc(self.sem, 1)
        self.n += 1
        return self.n

    def settle(self, upto=None):
        self.eng.wait_ge(self.sem, self.n if upto is None else upto)


def build(nc, x, meta, wd, w_uq, w_ukv, w_router, w1, w3, w2, prm, ident_d, tab_d, iota_d, out):
    with ExitStack() as ctx:
        A = ctx.enter_context(nc.sbuf_tensor("arena", [P, TOTAL], F32))
        PS = ctx.enter_context(nc.psum_tensor("PS", [P, 8, 512], F32))
        PF = PS[:, :, :].rearrange("p b c -> p (b c)")

        def sem(name):
            return ctx.enter_context(nc.semaphore(name))

        X = A[:, XOFF:XOFF + NT * D].rearrange("p (t d) -> p t d", t=NT)
        sm = Carve(A, SMALL, TOTAL)
        ident = sm(P)
        prm_s = sm(NPRM)
        wr = sm(KD * E).rearrange("p (k e) -> p k e", k=KD)
        iota = sm(S + NT)
        iota_row, iota_tok = iota[:, 0:S], iota[:, S:S + NT]
        ones = sm(1)
        eps = sm(1)
        stat = sm(9)
        rstd = sm(9)
        newt = sm(16)
        var = sm(16)
        ms = [sm(16), sm(16)]
        rs = [sm(16), sm(16)]
        nmax = sm(4)
        lsum = sm(32)
        krs = sm(5)
        linv = sm(32)
        rmask = sm(P)
        nrow = sm(64)
        TB = sm.at
        tab = sm(NTAB)

        def prm_c(name, i=0, n=1):
            a, _ = PRM[name]
            return prm_s[:, a + i:a + i + n]

        def tab_c(name):
            a, n = TAB[name]
            return tab[:, a:a + n]

        mcc, mss, rcc, rss = (tab_c(n).rearrange("p (t c) -> p t c", t=5) for n in ("mcc", "mss", "rcc", "rss"))
        bcc, bss = (tab_c(n).rearrange("p (t c) -> p t c", t=4) for n in ("bcc", "bss"))
        dec = tab_c("dec").rearrange("p (h c) -> p h c", h=RH)
        cm = tab_c("cm")

        c1 = Carve(A, 0, WS)
        UT = c1(KD * LT).rearrange("p (k c) -> p k c", k=KD)
        YT = A[:, 0:KD * S].rearrange("p (k c) -> p k c", k=KD)
        BUFA = c1(2400)
        U = [BUFA[:, 0:D], BUFA[:, D:2 * D]]
        SQ = BUFA[:, 0:1552]
        QSQ = BUFA[:, 0:1280]
        PB = [BUFA[:, 0:528], BUFA[:, 528:1056]]
        PTS = [BUFA[:, 1056:1696], BUFA[:, 1696:2336]]
        CQT = c1(2 * S)
        CKVT = c1(LT)
        MZ = c1(NT * 512)
        RQT = c1(2 * S).rearrange("p (j c) -> p j c", j=2)
        RKT = c1(2 * LT).rearrange("p (j c) -> p j c", j=2)
        RV = c1(5 * 256)
        UP0 = c1.at
        SRZ = c1(1024)
        XM = SRZ
        CU1 = c1(2 * (S + 2)).rearrange("p (b c) -> p b c", b=2)
        YR = CU1.rearrange("p b c -> p (b c)")[:, 0:1024]
        CG = c1(1028)[:, 0:1024].rearrange("p (b c) -> p b c", b=2)
        UPW = A[:, UP0:UP0 + 2 * 768 + 1024]
        CGF = CG.rearrange("p b c -> p (b c)")
        KR, KRQ, KRT = (CGF[:, 512 + 160 * i:672 + 160 * i].rearrange("p (t c) -> p t c", t=5) for i in range(3))
        QK0 = c1.at
        QTOK = [c1(768), c1(768)]
        KTOK = [c1(768), c1(768)]
        SD = [A[:, QK0:QK0 + 1792], BUFA[:, 0:1792]]
        YM = [A[:, QK0 + 1792:QK0 + 2304], A[:, QK0 + 2304:QK0 + 2816]]
        V1 = c1(5 * 512)
        QT = c1(MH * S).rearrange("p (h c) -> p h c", h=MH)
        KT = c1(MH * LT).rearrange("p (h c) -> p h c", h=MH)
        rq_a, rq_b = (c1(4 * 32).rearrange("p (t c) -> p t c", t=4) for _ in range(2))
        rk_a, rk_b = (c1(5 * 32).rearrange("p (t c) -> p t c", t=5) for _ in range(2))
        RT1, RT2 = c1(512), c1(512)
        SCR = c1(1024)
        KRG = c1(160).rearrange("p (t c) -> p t c", t=5)

        c2 = Carve(A, KD * LT, R2 + (N2 - 4) * D)
        U2f = c2(2048)
        U2 = [U2f[:, 0:D], U2f[:, D:2 * D]]
        UT2 = c2(KD * S).rearrange("p (k c) -> p k c", k=KD)
        CU2 = c2(4 * CW).rearrange("p (b c) -> p b c", b=4)
        CA = c2(4 * S).rearrange("p (b c) -> p b c", b=4)
        SCB = [c2(512), c2(512)]
        LV, LY, LA = c2(512), c2(512), c2(512)
        XN, XT1, XT2, XSQ = c2(512), c2(512), c2(512), c2(512)
        V2 = c2(NT * 512)
        QT2, KT2 = (c2(4 * S).rearrange("p (j c) -> p j c", j=4) for _ in range(2))
        SM = [c2(512), c2(512)]
        PT2 = [c2(512), c2(512)]
        YM2 = [c2(512), c2(512)]
        tq_a, tq_b, tk_a, tk_b = (c2(4 * 64).rearrange("p (t c) -> p t c", t=4) for _ in range(4))
        YT2 = A[:, R2 + (N2 - 4) * D:WS].rearrange("p (k c) -> p k c", k=KD)
        LN_ONES = c2(P)
        LSQ = U2f.rearrange("p (b c) -> p b c", b=4)

        W13 = [A[:, R13 + k * FF:R13 + (k + 1) * FF] for k in range(KD)]
        W2S = [A[:, R2 + i * D:R2 + (i + 1) * D] for i in range(N2)]
        H2N = A[:, WS + WSLOT:WS + WSLOT + NT * D].rearrange("p (t d) -> p t d", t=NT)
        ca = Carve(A, WS, WS + WSLOT)
        S1, HH = ca(FH), ca(FH)
        HT = ca(FJ * P).rearrange("p (j c) -> p j c", j=FJ)
        cb = Carve(A, TB, TOTAL)
        IDXB = cb(E * CAP)
        SEL = cb(NT * CAP).rearrange("p (t c) -> p t c", t=NT)
        G = cb(S)
        XE = cb(KD * CAP).rearrange("p (k c) -> p k c", k=KD)
        YE = cb(512)
        H2T = cb(D).rearrange("p (k c) -> p k c", k=KD)
        AFFT = cb(S)
        AFF = A[:, WS:WS + 64].rearrange("p (t e) -> p t e", t=NT)
        AEX = A[:, WS + 64:WS + 128].rearrange("p (t e) -> p t e", t=NT)
        A4, A4B = A[:, WS + 128:WS + 132], A[:, WS + 132:WS + 136]
        VAL = A[:, WS + 136:WS + 264]
        IDU = A[:, WS + 264:WS + 328].bitcast(U32)
        IDF = A[:, WS + 328:WS + 456]
        GT, IDT = cb(E), cb(E)
        RSC = A[:, WS + 512:WS + 512 + D]

        WSL = [A[:, WS + i * WSLOT:WS + (i + 1) * WSLOT] for i in range(2)]

        names = """cst_in tab_in gp_init gp_rope ustat u_ready ut_psum ut_ready lat_psum sq_ready lat_ready stat_psum lat_exp
        lat_rstd kr_psum kr_copied mz_psum mz_exp mz_free qk_psum qk_evac ms_ready ms_exp q_ready k_ready qT_psum
        kT_psum qT_evac kT_evac e_psum e_free rr_ready rrT_psum rrT_evac rz_exp f_psum cc_evac cx_done cz_exp cz_done
        conv_y rs_psum ret_s ro_psum ro_sq ro_ms ro_exp yr_ready yrT_psum yrT_evac s_psum nm_ready p_done pt_psum
        pt_evac pv_psum yo_free ym_ready yt_psum yt_evac op_psum xo_done ustat2 u2_ready ut2_psum ut2_ready
        pads f2_psum b_exp cu_done z_psum z_sq z_ms z_rs z_free zr_ready zT_psum zT_evac v_evac s2_psum nm2_ready
        p2_done pt2_psum pt2_evA pv2_psum ym2_ready yt2_psum yt2_evac cv_done mean_psum cen_done lsq_done
        var_psum lv_ready lrs_done ly_ready ly_exp y2_done op2_psum xo2_done rstat h2_ready h2T_psum h2T_ready lg_psum
        lg_sub lg_exp aff_ready affT_psum tk_ready tkT_psum gates_ready sel_ready gx_psum xe_ready s1_done hh_done
        w13_used w2_used ht_psum ht_evD ht_evA ye_ready sc_psum sc_add out_done act_own dve_own gp_own""".split()
        s = {n: sem(n) for n in names}
        x_in = [sem(f"x_in{i}") for i in range(5)]
        ws_in = [sem(f"ws_in{i}") for i in range(2)]
        w13_in = [sem(f"w13_in{i}") for i in range(KD)]
        w2_in = [sem(f"w2_in{i}") for i in range(N2)]

        ws_level, level = [], [0, 0]
        for g, (_, parts) in enumerate(GROUPS):
            level[g % 2] += 16 * len(parts)
            ws_level.append(level[g % 2])
        released = {0: ("lat_psum", 4), 1: ("mz_psum", 4), 2: ("e_psum", 5), 3: ("e_psum", 10), 4: ("f_psum", 4),
                    5: ("f_psum", 8), 6: ("op_psum", 4), 7: ("op_psum", 8), 8: ("f2_psum", 4), 9: ("f2_psum", 8),
                    10: ("z_psum", 4), 11: ("z_psum", 8), 12: ("z_psum", 12)}

        def group(g):
            n = sum(c for _, c in GROUPS[g][1])
            return WSL[g % 2][:, 0:KD * n].rearrange("p (k c) -> p k c", k=KD)

        def meta_pt(i):
            t = i // MH
            return PS[0:META, 4 + i % 2, (t + 1) * P:(t + 2) * P] if t < NT - 1 else PS[0:META, 6, 0:P]

        def toks(t):
            return (t * P, P) if t < NT else (S, META)

        block = ctx.enter_context(nc.Block())

        @block.sync
        def _(sp):
            def load_group(g):
                if g >= 2:
                    name, v = released[g - 2]
                    sp.wait_ge(s[name], v)
                at = 0
                for c, n in GROUPS[g][1]:
                    sp.dma_start(group(g)[:, :, at:at + n],
                                 wd[GROUPS[g][0]].rearrange("(k p) c -> p k c", p=P)[:, :, c:c + n]).then_inc(ws_in[g % 2], 16)
                    at += n

            sp.dma_start(X[:, 0, :], x[0:P, :]).then_inc(x_in[0], 16)
            sp.dma_start(ident, ident_d).then_inc(s["cst_in"], 16)
            sp.dma_start(prm_s, prm).then_inc(s["cst_in"], 16)
            for t in range(1, NT):
                sp.dma_start(X[:, t, :], x[t * P:(t + 1) * P, :]).then_inc(x_in[t], 16)
            sp.dma_start(XM[0:META, :], meta).then_inc(x_in[4], 16)
            load_group(0)
            sp.dma_start(tab, tab_d).then_inc(s["tab_in"], 16)
            load_group(1)
            sp.wait_ge(s["u_ready"], 5)
            sp.dma_start(UPW[:, 0:1536].rearrange("p (k c) -> p k c", k=2), w_uq.rearrange("(k p) c -> p k c", p=P)).then_inc(s["tab_in"], 16)
            sp.dma_start(UPW[:, 1536:2560], w_ukv).then_inc(s["tab_in"], 16)
            sp.dma_start(wr, w_router.rearrange("(k p) e -> p k e", p=P)).then_inc(s["tab_in"], 16)
            sp.dma_start(iota, iota_d).then_inc(s["tab_in"], 16)
            for g in range(2, len(GROUPS)):
                load_group(g)
            sp.wait_ge(s["yt2_evac"], 4)
            sp.wait_ge(s["y2_done"], 4)
            w1v = w1.rearrange("e (k p) f -> e k p f", p=P)
            w3v = w3.rearrange("e (k p) f -> e k p f", p=P)
            w2v = w2.rearrange("e (h j p) d -> e j h p d", h=2, p=P)

            def expert_loads(e, w1_first):
                for k in range(KD):
                    if not w1_first:
                        sp.wait_ge(s["w13_used"], e * (2 * KD) - KD + k + 1)
                    sp.dma_start(W13[k], w1v[e, k]).then_inc(w13_in[k], 16)
                if w1_first:
                    for i in range(N2 - 4):
                        sp.dma_start(W2S[i], w2v[e, i // 2, i % 2]).then_inc(w2_in[i], 16)
                    sp.wait_ge(s["op2_psum"], 8)
                    for i in range(N2 - 4, N2):
                        sp.dma_start(W2S[i], w2v[e, i // 2, i % 2]).then_inc(w2_in[i], 16)
                for k in range(KD):
                    sp.wait_ge(s["w13_used"], e * (2 * KD) + k + 1)
                    sp.dma_start(W13[k], w3v[e, k]).then_inc(w13_in[k], 16)
                for i in range(N2 if w1_first else 0, 2 * N2):
                    sp.wait_ge(s["w2_used"], e * (2 * N2) - N2 + i + 1)
                    sp.dma_start(W2S[i % N2], w2v[e, i // 2, i % 2]).then_inc(w2_in[i % N2], 16)

            expert_loads(0, True)
            with sp.Fori(1, E) as e:
                expert_loads(e, False)
            for n in range(2 * NT):
                sp.wait_ge(s["sc_add"], (E - 1) * 2 * NT + n + 1)
                t, d = n // 2, n % 2
                sp.dma_start(out[t * P:(t + 1) * P, d * 512:(d + 1) * 512], X[:, t, d * 512:(d + 1) * 512]).then_inc(s["out_done"], 16)
            sp.wait_ge(s["out_done"], 16 * 2 * NT)

        @block.gpsimd
        def _(gp):
            own = Own(gp, s["gp_own"])
            gp.memset(ones, 1.0)
            gp.memset(eps, EPS)
            gp.memset(stat, 1.0)
            gp.memset(rstd, 1.0)
            gp.memset(var, 1.0)
            gp.memset(rmask[0:1, 0:64], 1.0)
            gp.memset(rmask[0:1, 64:P], 0.0)
            gp.memset(nrow[0:1, :], NEG)
            gp.memset(ms[0], 1.0)
            gp.memset(ms[1], 1.0)
            gp.memset(KR, 0.0).then_inc(s["gp_init"], 1)
            gp.wait_ge(s["tab_in"], 80)
            gp.wait_ge(s["cst_in"], 32)
            qs = QH ** -0.5

            def gain(name, n, t):
                return prm_c(name, 0, n).unsqueeze(1).to_broadcast([P, t, n])

            gp.tensor_tensor(rq_a, mcc[:, 0:4, :], gain("qr", 32, 4), ALU.mult)
            gp.tensor_tensor(rq_b, mss[:, 0:4, :], gain("qrs", 32, 4), ALU.mult)
            gp.tensor_tensor(rk_a, mcc, gain("kr", 32, 5), ALU.mult)
            gp.tensor_tensor(rk_b, mss, gain("krs", 32, 5), ALU.mult)
            gp.tensor_scalar(prm_c("qn"), prm_c("qn"), qs, None, ALU.mult).then_inc(s["gp_rope"], 1)
            gp.wait_ge(s["op_psum"], 1)
            own(gp.tensor_tensor(tq_a, bcc, gain("q2", 64, 4), ALU.mult))
            own(gp.tensor_tensor(tq_b, bss, gain("q2s", 64, 4), ALU.mult))
            gp.tensor_tensor(tk_a, bcc, gain("k2", 64, 4), ALU.mult)
            gp.tensor_tensor(tk_b, bss, gain("k2s", 64, 4), ALU.mult)
            own.settle()
            own(gp.tensor_scalar(tq_a, tq_a, HD ** -0.5, None, ALU.mult))
            own(gp.tensor_scalar(tq_b, tq_b, HD ** -0.5, None, ALU.mult))
            own.settle()
            gp.memset(LN_ONES, 1.0 / S)
            gp.memset(CU2[:, :, 0:PAD], 0.0)
            gp.memset(CU2[:, :, PAD + S:CW], 0.0).then_inc(s["pads"], 1)

        @block.scalar
        def _(act):
            own = Own(act, s["act_own"])

            def rsqrt_seed(y, sums, inv_n):
                own(act.activation(y, sums, ACT.Ln, bias=eps[0:y.shape[0], :], scale=inv_n))
                own.settle()
                return act.activation(y, y, ACT.Exp, scale=-0.5)

            act.preload_act_table_set("natural_log_exp_and_others")
            act.wait_ge(s["gp_init"], 1)
            for t in range(5):
                _, n = toks(t)
                src = X[:, t, :] if t < NT else XM[0:META, :]
                act.wait_ge(x_in[t], 16)
                if t >= 2:
                    act.wait_ge(s["ut_psum"], t - 1)
                own(act.activation(U[t % 2][0:n, :], src, ACT.Square, accum_out=stat[0:n, t:t + 1]))
                own.settle()
                rsqrt_seed(rstd[0:n, t:t + 1], stat[0:n, t:t + 1], 1.0 / D).then_inc(s["ustat"], 1)
            for b in range(4):
                act.wait_ge(s["lat_psum"], b + 1)
                src = PS[:, 4 + b, :] if b < 3 else PS[:, 7, 0:META]
                act.activation(SQ[:, b * 512:b * 512 + src.shape[1]], src, ACT.Square).then_inc(s["sq_ready"], 1)
            act.wait_ge(s["ut_ready"], 5)
            act.wait_ge(s["stat_psum"], 1)
            own(act.activation(rstd[:, 0:4], PS[:, 7, 32:36], ACT.Ln, bias=eps, scale=1.0 / 256))
            own(act.activation(rstd[:, 4:8], PS[:, 7, 36:40], ACT.Ln, bias=eps, scale=1.0 / 128))
            own(act.activation(rstd[0:META, 8:9], PS[0:META, 7, 40:41], ACT.Ln, bias=eps[0:META, :], scale=1.0 / 128))
            own.settle()
            act.activation(rstd, rstd, ACT.Exp, scale=-0.5).then_inc(s["lat_exp"], 1)
            for t in range(NT):
                act.wait_ge(s["mz_psum"], t + 1)
                if t >= 2:
                    act.wait_ge(s["mz_free"], t - 1)
                act.activation(SCR[:, (t % 2) * 512:(t % 2) * 512 + 512], PS[:, t % 2, :], ACT.Exp, scale=-1.0).then_inc(s["mz_exp"], 1)
            act.wait_ge(s["lat_rstd"], 1)

            def evac(t):
                _, n = toks(t)
                act.wait_ge(s["qk_psum"], t + 1)
                if t >= 2:
                    act.wait_ge(s["kT_psum"], t - 1)
                if t >= 1:
                    act.wait_ge(s["ms_ready"], t)
                if t < NT:
                    q = PS[:, 3:5, 0:384]
                    act.activation(QTOK[t % 2].rearrange("p (b c) -> p b c", b=2), q, ACT.Copy, scale=rstd[:, t:t + 1])
                    act.activation(QSQ[:, 0:768].rearrange("p (b c) -> p b c", b=2), q, ACT.Square, scale=rstd[:, t:t + 1])
                kv = PF[0:n, 5 * 512:7 * 512].rearrange("p (h c) -> p h c", h=MH)
                r = rstd[0:n, 4 + t:5 + t]
                act.activation(KTOK[t % 2][0:n, :].rearrange("p (h c) -> p h c", h=MH)[:, :, 0:NOPE], kv[:, :, 0:NOPE], ACT.Copy, scale=r)
                act.activation(QSQ[0:n, 768:1280].rearrange("p (h c) -> p h c", h=MH), kv[:, :, 0:NOPE], ACT.Square, scale=r)
                act.activation(V1[0:n, t * 512:(t + 1) * 512].rearrange("p (h c) -> p h c", h=MH), kv[:, :, NOPE:128], ACT.Copy,
                               scale=r).then_inc(s["qk_evac"], 1)

            def head_stats(t):
                _, n = toks(t)
                act.wait_ge(s["ms_ready"], t + 1)
                if t >= 2:
                    act.wait_ge(s["k_ready"], t - 1)
                a = 0 if t < NT else 8
                rsqrt_seed(rs[t % 2][0:n, a:16], ms[t % 2][0:n, a:16], 1.0 / QH).then_inc(s["ms_exp"], 1)

            def qT_out(t):
                act.wait_ge(s["qT_psum"], t + 1)
                for f in range(2):
                    i = act.activation(QT[0:QH, 4 * f:4 * f + 4, t * P:(t + 1) * P],
                                       PS[0:QH, f, :].rearrange("p (h c) -> p h c", h=4), ACT.Copy, scale=prm_c("qn")[0:QH, :])
                i.then_inc(s["qT_evac"], 1)

            def rrT_out(t):
                c, n = toks(t)
                act.wait_ge(s["rrT_psum"], t + 1)
                ps = PS[:, 0, :].rearrange("p (j c) -> p j c", j=4)
                if t < NT:
                    act.activation(RQT[:, :, c:c + n], ps[:, 0:2, :], ACT.Copy)
                act.activation(RKT[:, :, c:c + n], ps[:, 2:4, 0:n], ACT.Copy).then_inc(s["rrT_evac"], 1)

            evac(0), head_stats(0), evac(1), head_stats(1), qT_out(0), evac(2), head_stats(2)
            rrT_out(0), qT_out(1), evac(3), head_stats(3), rrT_out(1), qT_out(2), evac(4), head_stats(4)
            rrT_out(2), qT_out(3), rrT_out(3), rrT_out(4)
            for t in range(NT):
                act.wait_ge(s["e_psum"], 6 + t)
                b = [2, 7][(5 + t) % 2]
                if t >= 2:
                    act.wait_ge(s["e_free"], 4 + t)
                act.activation(RV[:, t * 256:(t + 1) * 256], PS[:, b, 0:256], ACT.Copy)
                act.activation(SCR[:, (t % 2) * 256:(t % 2) * 256 + 256], PS[:, b, 256:512], ACT.Exp, scale=-1.0).then_inc(s["rz_exp"], 1)
            for b in range(2):
                act.wait_ge(s["f_psum"], 2 * b + 1)
                act.activation(CU1[:, b, 0:2], PS[:, 2 * b, 0:2], ACT.Copy)
                act.activation(CU1[:, b, 2:S + 2], PS[:, 3 + 2 * b, :], ACT.Copy).then_inc(s["cc_evac"], 1)
            act.wait_ge(s["e_free"], 9)
            for b in range(2):
                act.wait_ge(s["f_psum"], 4 + 2 * b + 1)
                act.activation(SCR[:, b * 512:b * 512 + 512], PS[:, 3 + 2 * b, :], ACT.Exp, scale=-1.0).then_inc(s["cz_exp"], 1)
            act.wait_ge(s["ro_psum"], RH)
            act.wait_ge(s["cz_done"], 2)
            act.activation(SCR, PF[:, 6 * 512:8 * 512], ACT.Square).then_inc(s["ro_sq"], 1)
            act.wait_ge(s["ro_ms"], 1)
            rsqrt_seed(rs[0], ms[0], 1.0 / RD).then_inc(s["ro_exp"], 1)
            def probs(i):
                t, b = i // MH, 2 * (i % 2)
                n = (t + 1) * P + META
                act.wait_ge(s["nm_ready"], i + 1)
                if i >= 2:
                    act.wait_ge(s["pt_psum"], i - 1)
                act.activation(PB[i % 2][:, 0:n], PF[:, b * 512:b * 512 + n], ACT.Exp, bias=nmax[:, i % 4:i % 4 + 1],
                               accum_out=lsum[:, i:i + 1]).then_inc(s["p_done"], 1)

            def yt_out(t):
                act.wait_ge(s["yt_psum"], t + 1)
                act.activation(YT[:, 2:6, t * P:(t + 1) * P], PS[:, 3 if t == 3 else 1, :].rearrange("p (j c) -> p j c", j=4), ACT.Copy)\
                    .then_inc(s["yt_evac"], 1)

            act.wait_ge(s["ro_psum"], RH)
            for i in range(NT * MH):
                probs(i)
                if i in (MH + 3, 2 * MH + 3):
                    yt_out(i // MH - 1)
                if i == 2:
                    act.wait_ge(s["yrT_psum"], 1)
                    for j in range(2):
                        ins = act.activation(YT[:, 6 + j, :], PS[:, 1 + 2 * j, :], ACT.Copy)
                    ins.then_inc(s["yrT_evac"], 1)
            yt_out(NT - 2)
            yt_out(NT - 1)

            for t in range(NT):
                act.wait_ge(s["xo_done"], NT + 1 + t)
                if t >= 2:
                    act.wait_ge(s["ut2_psum"], t - 1)
                own(act.activation(U2[t % 2], X[:, t, :], ACT.Square, accum_out=stat[:, t:t + 1]))
                own.settle()
                rsqrt_seed(rstd[:, t:t + 1], stat[:, t:t + 1], 1.0 / D).then_inc(s["ustat2"], 1)
            for j in range(4):
                act.wait_ge(s["f2_psum"], 2 * j + 1)
                if j >= 2:
                    act.wait_ge(s["cu_done"], j - 1)
                act.activation(SCB[j % 2], PS[:, (2 * j) % 4, :], ACT.Exp, scale=-1.0).then_inc(s["b_exp"], 1)

            def zT_out(i):
                t = i % NT
                act.wait_ge(s["zT_psum"], i + 1)
                dst = QT2 if i < NT else KT2
                act.activation(dst[:, :, t * P:(t + 1) * P], PS[:, i % 2, :].rearrange("p (j c) -> p j c", j=4), ACT.Copy)\
                    .then_inc(s["zT_evac"], 1)

            for i in range(2 * NT):
                act.wait_ge(s["z_psum"], i + 1)
                if i >= 1:
                    act.wait_ge(s["z_ms"], i)
                act.activation(XSQ, PS[:, 4 + i % 4, :], ACT.Square).then_inc(s["z_sq"], 1)
                act.wait_ge(s["z_ms"], i + 1)
                rsqrt_seed(rs[i % 2][:, 0:8], ms[i % 2][:, 0:8], 1.0 / HD).then_inc(s["z_rs"], 1)
                if i >= 1:
                    zT_out(i - 1)
            zT_out(2 * NT - 1)
            for t in range(NT):
                act.wait_ge(s["z_psum"], 2 * NT + 1 + t)
                act.activation(V2[:, t * 512:(t + 1) * 512], PS[:, 4 + t % 4, :], ACT.Copy).then_inc(s["v_evac"], 1)

            def probs2(i):
                act.wait_ge(s["nm2_ready"], i + 1)
                act.activation(SM[i % 2], SM[i % 2], ACT.Exp, scale=-1.0, bias=nmax[:, i % 4:i % 4 + 1],
                               accum_out=lsum[:, i:i + 1]).then_inc(s["p2_done"], 1)

            def pt2_out(i):
                act.wait_ge(s["pt2_psum"], i + 1)
                if i >= 2:
                    act.wait_ge(s["pv2_psum"], i - 1)
                act.activation(PT2[i % 2], PS[:, 2 + i % 2, :], ACT.Copy).then_inc(s["pt2_evA"], 1)

            def yt2_out(t):
                act.wait_ge(s["yt2_psum"], t + 1)
                act.activation(YT2[:, 0:4, t * P:(t + 1) * P], PS[:, 6, :].rearrange("p (j c) -> p j c", j=4), ACT.Copy)\
                    .then_inc(s["yt2_evac"], 1)

            for i in range(NT * H2):
                probs2(i)
                if i >= 1:
                    pt2_out(i - 1)
                if i % H2 == 3 and i > H2:
                    yt2_out(i // H2 - 1)
                if i == LN_AT + 1:
                    for j in range(4):
                        act.wait_ge(s["cen_done"], j + 1)
                        act.activation(LSQ[:, j, :], CA[:, j, :], ACT.Square).then_inc(s["lsq_done"], 1)
                if i == LN_AT + 3:
                    act.wait_ge(s["lv_ready"], 1)
                    own(act.activation(LY, LV, ACT.Ln))
                    own.settle()
                    act.activation(LY, LY, ACT.Exp, scale=-0.5).then_inc(s["lrs_done"], 1)
                if LN_AT + 5 <= i < LN_AT + 9:
                    j = i - LN_AT - 5
                    act.wait_ge(s["ly_ready"], j + 1)
                    if j >= 2:
                        act.wait_ge(s["y2_done"], j - 1)
                    act.activation(SCB[j % 2], CA[:, j, :], ACT.Exp, scale=-1.0).then_inc(s["ly_exp"], 1)
            pt2_out(NT * H2 - 1)
            yt2_out(NT - 1)

            act.wait_ge(s["op2_psum"], 8)
            for t in range(NT):
                act.wait_ge(s["xo2_done"], NT + 1 + t)
                own(act.activation(RSC, X[:, t, :], ACT.Square, accum_out=stat[:, t:t + 1]))
                own.settle()
                rsqrt_seed(rstd[:, t:t + 1], stat[:, t:t + 1], 1.0 / D).then_inc(s["rstat"], 1)
            act.wait_ge(s["lg_sub"], 1)
            act.activation(AEX, AEX, ACT.Exp).then_inc(s["lg_exp"], 1)
            act.preload_act_table(ACT.Silu)

            def expert(e, first):
                act.wait_ge(s["w13_used"], e * (2 * KD) + KD)
                if not first:
                    act.wait_ge(s["hh_done"], e)
                act.activation(S1, PF[:, 0:FH], ACT.Silu).then_inc(s["s1_done"], 1)
                act.wait_ge(s["ht_psum"], e + 1)
                act.activation(HT[:, 0:4, :], PF[:, 0:4 * P].rearrange("p (j c) -> p j c", j=4), ACT.Copy).then_inc(s["ht_evA"], 1)

            expert(0, True)
            with act.Fori(1, E) as e:
                expert(e, False)

        @block.vector
        def _(dve):
            own = Own(dve, s["dve_own"])

            def refine(y, sums, inv_n, have_v=None, signal=None):
                n, w = y.shape
                v, a = var[0:n, 0:w], newt[0:n, 0:w]
                if have_v is None:
                    own(dve.tensor_scalar(v, sums, inv_n, EPS, ALU.mult, ALU.add))
                own(dve.tensor_tensor(a, y, y, ALU.mult))
                own.settle()
                own(dve.scalar_tensor_tensor(a, a, -0.5, v, ALU.mult, ALU.mult))
                own.settle()
                i = dve.scalar_tensor_tensor(y, a, 1.5, y, ALU.add, ALU.mult)
                if signal:
                    i.then_inc(s[signal], 1)
                else:
                    own(i)
                    own.settle()

            def bc(ap, n):
                return ap.unsqueeze(2).to_broadcast([ap.shape[0], ap.shape[1], n])

            def rows(ap, h):
                return ap.unsqueeze(1).to_broadcast([ap.shape[0], h, ap.shape[1]])

            dve.wait_ge(s["gp_init"], 1)
            dve.wait_ge(s["cst_in"], 32)
            for t in range(6):
                if t < 5:
                    _, n = toks(t)
                    dve.wait_ge(s["ustat"], t + 1)
                    refine(rstd[0:n, t:t + 1], stat[0:n, t:t + 1], 1.0 / D)
                    src = X[:, t, :] if t < NT else XM[0:META, :]
                    dve.tensor_scalar(U[t % 2][0:n, :], src, rstd[0:n, t:t + 1], None, ALU.mult).then_inc(s["u_ready"], 1)
                if t >= 1:
                    c, n = toks(t - 1)
                    dve.wait_ge(s["ut_psum"], t)
                    for f in range(2):
                        i = dve.tensor_tensor(UT[:, 4 * f:4 * f + 4, c:c + n],
                                              PS[:, 2 * ((t - 1) % 2) + f, :].rearrange("p (k c) -> p k c", k=4)[:, :, 0:n],
                                              bc(prm_c("lnw", 4 * f, 4), n), ALU.mult)
                    i.then_inc(s["ut_ready"], 1)
            for b in range(4):
                dve.wait_ge(s["sq_ready"], b + 1)
                if b < 2:
                    i = dve.tensor_scalar(CQT[:, b * S:(b + 1) * S], PS[:, 4 + b, :], prm_c("qan", b), None, ALU.mult)
                elif b == 2:
                    i = dve.tensor_scalar(CKVT[:, 0:S], PS[:, 6, :], prm_c("kvan"), None, ALU.mult)
                else:
                    i = dve.tensor_scalar(CKVT[:, S:LT], PS[:, 7, 0:META], prm_c("kvan"), None, ALU.mult)
                i.then_inc(s["lat_ready"], 1)
            dve.wait_ge(s["kr_psum"], 1)
            dve.wait_ge(s["gp_rope"], 1)
            own(dve.tensor_copy(KR[:, 0:4, :], PS[:, 2, 0:128].rearrange("p (t c) -> p t c", t=4)))
            dve.tensor_copy(KR[0:META, 4, :], PS[0:META, 2, 128:160]).then_inc(s["kr_copied"], 1)
            dve.wait_ge(s["kr_copied"], 1)
            own(dve.tensor_tensor(KRQ, KR, KR, ALU.mult))
            own.settle()
            own(dve.tensor_reduce(krs, KRQ, AX.X, ALU.add))
            own.settle()
            own(dve.tensor_tensor(KRQ[:, :, 0:16], KR[:, :, 16:32], rk_b[:, :, 0:16], ALU.mult))
            own(dve.tensor_tensor(KRQ[:, :, 16:32], KR[:, :, 0:16], rk_b[:, :, 16:32], ALU.mult))
            own(dve.tensor_tensor(KRT, KR, rk_a, ALU.mult))
            own.settle()
            own(dve.tensor_tensor(KRG, KRQ, KRT, ALU.add))
            dve.wait_ge(s["lat_exp"], 1)
            own(dve.tensor_scalar(var[:, 0:4], PS[:, 7, 32:36], 1.0 / 256, EPS, ALU.mult, ALU.add))
            own(dve.tensor_scalar(var[:, 4:8], PS[:, 7, 36:40], 1.0 / 128, EPS, ALU.mult, ALU.add))
            own(dve.tensor_scalar(var[0:META, 8:9], PS[0:META, 7, 40:41], 1.0 / 128, EPS, ALU.mult, ALU.add))
            refine(rstd, None, None, have_v=True, signal="lat_rstd")

            def silu(e, z, dst):
                own(dve.tensor_scalar(e, e, 1.0, None, ALU.add))
                own.settle()
                own(dve.reciprocal(e, e))
                own.settle()
                return dve.tensor_tensor(dst, e, z, ALU.mult)

            for t in range(NT):
                dve.wait_ge(s["mz_exp"], t + 1)
                silu(SCR[:, (t % 2) * 512:(t % 2) * 512 + 512], PS[:, t % 2, :], MZ[:, t * 512:(t + 1) * 512]).then_inc(s["mz_free"], 1)

            def reduce_heads(t):
                _, n = toks(t)
                dve.wait_ge(s["qk_evac"], t + 1)
                if t >= 2:
                    dve.wait_ge(s["ms_exp"], t - 1)
                m = ms[t % 2]
                own(dve.tensor_reduce(m[0:n, 8:16], QSQ[0:n, 768:1280].rearrange("p (h c) -> p h c", h=MH), AX.X, ALU.add))
                if t < NT:
                    own(dve.tensor_reduce(m[:, 0:8], QSQ[:, 0:768].rearrange("p (h c) -> p h c", h=MH), AX.X, ALU.add))
                own.settle()
                dve.tensor_scalar(m[0:n, 8:16], m[0:n, 8:16], krs[0:n, t:t + 1], None, ALU.add).then_inc(s["ms_ready"], 1)

            def apply_heads(t):
                _, n = toks(t)
                dve.wait_ge(s["ms_exp"], t + 1)
                dve.wait_ge(s["ms_ready"], t + 1)
                r = rs[t % 2]
                a = 0 if t < NT else 8
                refine(r[0:n, a:16], ms[t % 2][0:n, a:16], 1.0 / QH)
                if t < NT:
                    q = QTOK[t % 2].rearrange("p (h c) -> p h c", h=MH)
                    own(dve.tensor_tensor(q, q, bc(r[:, 0:8], QH), ALU.mult))
                    own.settle()
                    if t >= 1:
                        dve.wait_ge(s["rrT_psum"], t)
                    t1 = RT1[:, 0:256].rearrange("p (h c) -> p h c", h=MH)
                    t2 = RT2[:, 0:256].rearrange("p (h c) -> p h c", h=MH)
                    own(dve.tensor_tensor(t1, q[:, :, 64:96], rows(rq_a[:, t, :], MH), ALU.mult))
                    own(dve.tensor_tensor(t2[:, :, 0:16], q[:, :, 80:96], rows(rq_b[:, t, 0:16], MH), ALU.mult))
                    own(dve.tensor_tensor(t2[:, :, 16:32], q[:, :, 64:80], rows(rq_b[:, t, 16:32], MH), ALU.mult))
                    own.settle()
                    dve.tensor_tensor(q[:, :, 64:96], t1, t2, ALU.add).then_inc(s["q_ready"], 1)
                k = KTOK[t % 2][0:n, :].rearrange("p (h c) -> p h c", h=MH)
                own(dve.tensor_tensor(k[:, :, 0:NOPE], k[:, :, 0:NOPE], bc(r[0:n, 8:16], NOPE), ALU.mult))
                dve.tensor_tensor(k[:, :, 64:96], rows(KRG[0:n, t, :], MH), bc(r[0:n, 8:16], ROPE), ALU.mult).then_inc(s["k_ready"], 1)

            def kT_out(t):
                c, n = toks(t)
                dve.wait_ge(s["kT_psum"], t + 1)
                for f in range(2):
                    i = dve.tensor_scalar(KT[0:QH, 4 * f:4 * f + 4, c:c + n],
                                          PS[0:QH, f, :].rearrange("p (h c) -> p h c", h=4)[:, :, 0:n], prm_c("kn")[0:QH, :], None, ALU.mult)
                i.then_inc(s["kT_evac"], 1)

            def rotate(t):
                _, n = toks(t)
                dve.wait_ge(s["e_psum"], t + 1)
                if t >= 1:
                    dve.wait_ge(s["rrT_psum"], t)
                if t < NT:
                    dve.wait_ge(s["q_ready"], t + 1)
                b = [2, 7][t % 2]
                h = 8 if t < NT else 4
                o = 0 if t < NT else 256
                src = PS[0:n, b, o:512].rearrange("p (h c) -> p h c", h=h)
                t1 = RT1[0:n, o:512].rearrange("p (h c) -> p h c", h=h)
                t2 = RT2[0:n, o:512].rearrange("p (h c) -> p h c", h=h)
                own(dve.tensor_tensor(t1, src, rows(rcc[0:n, t, :], h), ALU.mult))
                own(dve.tensor_tensor(t2[:, :, 0:32], src[:, :, 32:64], rows(rss[0:n, t, 0:32], h), ALU.mult))
                dve.tensor_tensor(t2[:, :, 32:64], src[:, :, 0:32], rows(rss[0:n, t, 32:64], h), ALU.mult).then_inc(s["e_free"], 1)
                dve.wait_ge(s["e_free"], t + 1)
                own.settle()
                dve.tensor_tensor(t1, t1, t2, ALU.add).then_inc(s["rr_ready"], 1)

            reduce_heads(0), reduce_heads(1), apply_heads(0), rotate(0), kT_out(0), reduce_heads(2)
            apply_heads(1), rotate(1), kT_out(1), reduce_heads(3), apply_heads(2), rotate(2), kT_out(2), reduce_heads(4)
            apply_heads(3), rotate(3), kT_out(3), apply_heads(4), rotate(4), kT_out(4)
            for t in range(NT):
                dve.wait_ge(s["rz_exp"], t + 1)
                silu(SCR[:, (t % 2) * 256:(t % 2) * 256 + 256], PS[:, [2, 7][(5 + t) % 2], 256:512],
                     SRZ[:, t * 256:(t + 1) * 256]).then_inc(s["e_free"], 1)
            dve.wait_ge(s["e_psum"], 10)
            dve.tensor_copy(RV[0:META, 1024:1280], PS[0:META, [2, 7][9 % 2], 0:256]).then_inc(s["e_free"], 1)
            for b in range(2):
                dve.wait_ge(s["cc_evac"], b + 1)
                dve.wait_ge(s["f_psum"], 2 * b + 2)
                own(dve.tensor_tensor(CU1[:, b, 0:2], CU1[:, b, 0:2], PS[:, [1, 7][b], 0:2], ALU.mult))
                dve.tensor_tensor(CU1[:, b, 2:S + 2], CU1[:, b, 2:S + 2], PS[:, 4 + 2 * b, :], ALU.mult).then_inc(s["cx_done"], 1)
            for b in range(2):
                dve.wait_ge(s["cz_exp"], b + 1)
                own(silu(SCR[:, b * 512:b * 512 + 512], PS[:, 3 + 2 * b, :], CG[:, b, :]))
                own.settle()
                dve.wait_ge(s["f_psum"], 4 + 2 * b + 2)
                dve.tensor_tensor(CG[:, b, :], CG[:, b, :], PS[:, 4 + 2 * b, :], ALU.mult).then_inc(s["cz_done"], 1)
            dve.wait_ge(s["cx_done"], 2)
            dve.wait_ge(s["cz_done"], 2)
            dve.wait_ge(s["rrT_psum"], 5)
            acc = [RT1, RT2]
            for j in range(3):
                for b in range(2):
                    w = prm_c("cw", b * 3 + j)
                    if j == 0:
                        own(dve.tensor_scalar(acc[b], CU1[:, b, 0:S], w, prm_c("cb", b), ALU.mult, ALU.add))
                    else:
                        own.settle(own.n - 1)
                        own(dve.scalar_tensor_tensor(acc[b], CU1[:, b, j:j + S], w, acc[b], ALU.mult, ALU.add))
            own.settle()
            for b in range(2):
                dve.tensor_tensor(YT[:, b, :], acc[b], CG[:, b, :], ALU.mult).then_inc(s["conv_y"], 1)
            dve.wait_ge(s["kT_psum"], 5)
            for h in range(RH):
                sd = SD[h % 2]
                if h >= 2:
                    dve.wait_ge(s["ro_psum"], h - 1)
                for b in range(5):
                    i = 5 * h + b
                    dve.wait_ge(s["rs_psum"], i + 1)
                    if b < NT:
                        n = S - b * P
                        o = [0, 512, 896, 1152][b]
                        ins = dve.tensor_tensor(sd[:, o:o + n], PS[:, i % 4, 0:n], dec[:, h, 0:n], ALU.mult)
                    else:
                        ins = dve.tensor_tensor(sd[0:META, 1280:1792], PS[0:META, i % 4, :], dec[0:META, h, META:LT], ALU.mult)
                    ins.then_inc(s["ret_s"], 1)
            dve.wait_ge(s["ro_sq"], 1)
            dve.tensor_reduce(ms[0], SCR.rearrange("p (g e) -> p g e", g=16), AX.X, ALU.add).then_inc(s["ro_ms"], 1)
            dve.wait_ge(s["ro_exp"], 1)
            dve.wait_ge(s["ro_ms"], 1)
            refine(rs[0], ms[0], 1.0 / RD)
            yr = YR.rearrange("p (g e) -> p g e", g=16)
            own(dve.tensor_tensor(yr, PF[:, 6 * 512:8 * 512].rearrange("p (g e) -> p g e", g=16), bc(rs[0], RD), ALU.mult))
            own.settle()
            own(dve.tensor_tensor(yr, yr, rows(prm_c("retn", 0, 64), 16), ALU.mult))
            own.settle()
            dve.wait_ge(s["e_free"], 10)
            dve.tensor_tensor(YR, YR, SRZ, ALU.mult).then_inc(s["yr_ready"], 1)

            def row_max(i):
                t, b = i // MH, 2 * (i % 2)
                n = (t + 1) * P + META
                dve.wait_ge(s["s_psum"], i + 1)
                if i >= 4:
                    dve.wait_ge(s["p_done"], i - 3)
                dve.tensor_reduce(nmax[:, i % 4:i % 4 + 1], PF[:, b * 512:b * 512 + n], AX.X, ALU.max, negate=True).then_inc(s["nm_ready"], 1)

            def pt_out(i):
                n = (i // MH + 1) * P
                dve.wait_ge(s["pt_psum"], i + 1)
                if i >= 2:
                    dve.wait_ge(s["pv_psum"], i - 1)
                dve.tensor_copy(PTS[i % 2][:, 0:n], PS[:, 4 + i % 2, 0:n])
                dve.tensor_copy(PTS[i % 2][0:META, 512:640], meta_pt(i)).then_inc(s["pt_evac"], 1)

            def tile_out(t):
                dve.wait_ge(s["pv_psum"], MH * (t + 1))
                li = linv[:, MH * t:MH * (t + 1)]
                own(dve.reciprocal(li, lsum[:, MH * t:MH * (t + 1)]))
                own.settle()
                if t >= 2:
                    dve.wait_ge(s["yt_psum"], t - 1)
                y = YM[t % 2].rearrange("p (h c) -> p h c", h=MH)
                dve.tensor_tensor(y, PS[:, 6 + t % 2, :].rearrange("p (h c) -> p h c", h=MH), bc(li, VH), ALU.mult).then_inc(s["yo_free"], 1)
                dve.wait_ge(s["yo_free"], t + 1)
                dve.tensor_tensor(YM[t % 2], YM[t % 2], MZ[:, t * 512:(t + 1) * 512], ALU.mult).then_inc(s["ym_ready"], 1)

            for i in range(NT * MH):
                row_max(i)
                if i >= 1:
                    pt_out(i - 1)
                if i % MH == 0 and i > 0:
                    tile_out(i // MH - 1)
            pt_out(NT * MH - 1)
            tile_out(NT - 1)
            for i in range(2 * NT):
                n, t = i // NT, i % NT
                dve.wait_ge(s["op_psum"], i + 1)
                xs = X[:, t, n * 512:(n + 1) * 512]
                dve.tensor_tensor(xs, xs, PS[:, i % 4, :], ALU.add).then_inc(s["xo_done"], 1)

            for t in range(NT + 1):
                if t < NT:
                    dve.wait_ge(s["ustat2"], t + 1)
                    refine(rstd[:, t:t + 1], stat[:, t:t + 1], 1.0 / D)
                    dve.tensor_scalar(U2[t % 2], X[:, t, :], rstd[:, t:t + 1], None, ALU.mult).then_inc(s["u2_ready"], 1)
                if t >= 1:
                    c = (t - 1) * P
                    dve.wait_ge(s["ut2_psum"], t)
                    for f in range(2):
                        i = dve.tensor_tensor(UT2[:, 4 * f:4 * f + 4, c:c + P],
                                              PS[:, 4 + 2 * ((t - 1) % 2) + f, :].rearrange("p (k c) -> p k c", k=4),
                                              bc(prm_c("n1g", 4 * f, 4), P), ALU.mult)
                    i.then_inc(s["ut2_ready"], 1)
            dve.wait_ge(s["pads"], 1)
            for j in range(4):
                dve.wait_ge(s["b_exp"], j + 1)
                dve.wait_ge(s["f2_psum"], 2 * j + 2)
                silu(SCB[j % 2], PS[:, (2 * j + 1) % 4, :], CU2[:, j, PAD:PAD + S]).then_inc(s["cu_done"], 1)

            def taps_ops():
                for pair in ((0, 1), (2, 3)):
                    for j in range(TAPS):
                        for b in pair:
                            w = prm_c("dw", b * TAPS + j)
                            if j == 0:
                                dve.wait_ge(s["cu_done"], 4)
                                own(dve.tensor_scalar(CA[:, b, :], CU2[:, b, 0:S], w, prm_c("dwb", b), ALU.mult, ALU.add))
                            else:
                                own.settle(last[b])
                                i = dve.scalar_tensor_tensor(CA[:, b, :], CU2[:, b, j:j + S], w, CA[:, b, :], ALU.mult, ALU.add)
                                if (b, j) == (3, TAPS - 1):
                                    i.then_inc(s["cv_done"], 1)
                                    return
                                own(i)
                            last[b] = own.n
                            yield

            last = {}
            ops = taps_ops()

            def some_taps(n):
                for _ in range(n):
                    next(ops, None)

            for i in range(2 * NT):
                t = i % NT
                ta, tb = (tq_a, tq_b) if i < NT else (tk_a, tk_b)
                dve.wait_ge(s["z_sq"], i + 1)
                if i >= 2:
                    dve.wait_ge(s["z_rs"], i - 1)
                dve.tensor_reduce(ms[i % 2][:, 0:8], XSQ.rearrange("p (h c) -> p h c", h=H2), AX.X, ALU.add).then_inc(s["z_ms"], 1)
                some_taps(TAPS_PER_TILE)
                dve.wait_ge(s["z_rs"], i + 1)
                dve.wait_ge(s["z_ms"], i + 1)
                refine(rs[i % 2][:, 0:8], ms[i % 2][:, 0:8], 1.0 / HD)
                xn = XN.rearrange("p (h c) -> p h c", h=H2)
                t1 = XT1.rearrange("p (h c) -> p h c", h=H2)
                t2 = XT2.rearrange("p (h c) -> p h c", h=H2)
                dve.tensor_tensor(xn, PS[:, 4 + i % 4, :].rearrange("p (h c) -> p h c", h=H2), bc(rs[i % 2][:, 0:8], HD), ALU.mult)\
                    .then_inc(s["z_free"], 1)
                dve.wait_ge(s["z_free"], i + 1)
                if i >= 1:
                    dve.wait_ge(s["zT_psum"], i)
                own(dve.tensor_tensor(t1, xn, rows(ta[:, t, :], H2), ALU.mult))
                own(dve.tensor_tensor(t2[:, :, 0:32], xn[:, :, 32:64], rows(tb[:, t, 0:32], H2), ALU.mult))
                own(dve.tensor_tensor(t2[:, :, 32:64], xn[:, :, 0:32], rows(tb[:, t, 32:64], H2), ALU.mult))
                own.settle()
                dve.tensor_tensor(t1, t1, t2, ALU.add).then_inc(s["zr_ready"], 1)

            def row_max2(i):
                t = i // H2
                dve.wait_ge(s["s2_psum"], i + 1)
                if i >= 2:
                    dve.wait_ge(s["pt2_psum"], i - 1)
                if i >= 4:
                    dve.wait_ge(s["p2_done"], i - 3)
                dve.tensor_tensor_reduce(out=SM[i % 2], in0=PS[:, i % 2, :], in1=cm[:, S - P - t * P:2 * S - P - t * P], scale=-1.0,
                                         scalar=3.0e38, op0=ALU.add, op1=ALU.min, accum_out=nmax[:, i % 4:i % 4 + 1]).then_inc(s["nm2_ready"], 1)

            def tile_out2(t):
                dve.wait_ge(s["pv2_psum"], H2 * (t + 1))
                li = linv[:, H2 * t:H2 * (t + 1)]
                own(dve.reciprocal(li, lsum[:, H2 * t:H2 * (t + 1)]))
                own.settle()
                if t >= 2:
                    dve.wait_ge(s["yt2_psum"], t - 1)
                dve.tensor_tensor(YM2[t % 2].rearrange("p (h c) -> p h c", h=H2), PS[:, 4 + t % 2, :].rearrange("p (h c) -> p h c", h=H2),
                                  bc(li, HD), ALU.mult).then_inc(s["ym2_ready"], 1)

            for i in range(NT * H2):
                row_max2(i)
                if i % H2 == 1 and i > H2:
                    tile_out2(i // H2 - 1)
                if i < LN_AT:
                    some_taps(TAPS_PER_HEAD)
                if i == LN_AT - 1:
                    for _ in ops:
                        pass
                if i == LN_AT + 1:
                    dve.wait_ge(s["mean_psum"], 1)
                    dve.wait_ge(s["cv_done"], 1)
                    for j in range(4):
                        dve.tensor_tensor(CA[:, j, :], CA[:, j, :], PS[:, 7, :], ALU.subtract).then_inc(s["cen_done"], 1)
                if i == LN_AT + 3:
                    dve.wait_ge(s["var_psum"], 1)
                    dve.tensor_scalar(LV, PS[:, 7, :], EPS, None, ALU.add).then_inc(s["lv_ready"], 1)
                if i == LN_AT + 4:
                    dve.wait_ge(s["lrs_done"], 1)
                    own(dve.tensor_tensor(LA, LY, LY, ALU.mult))
                    own.settle()
                    own(dve.scalar_tensor_tensor(LA, LA, -0.5, LV, ALU.mult, ALU.mult))
                    own.settle()
                    own(dve.scalar_tensor_tensor(LY, LA, 1.5, LY, ALU.add, ALU.mult))
                if LN_AT + 5 <= i < LN_AT + 9:
                    j = i - LN_AT - 5
                    own.settle()
                    dve.wait_ge(s["cen_done"], 4)
                    dve.wait_ge(s["lsq_done"], 4)
                    own(dve.tensor_tensor(CA[:, j, :], CA[:, j, :], LY, ALU.mult))
                    own.settle()
                    dve.tensor_scalar(CA[:, j, :], CA[:, j, :], prm_c("lng", j), prm_c("lnb", j), ALU.mult, ALU.add).then_inc(s["ly_ready"], 1)
                if LN_AT + 6 <= i < LN_AT + 10:
                    j = i - LN_AT - 6
                    dve.wait_ge(s["ly_exp"], j + 1)
                    silu(SCB[j % 2], CA[:, j, :], YT2[:, 4 + j, :]).then_inc(s["y2_done"], 1)
            tile_out2(NT - 1)
            for i in range(2 * NT):
                n, t = i // NT, i % NT
                dve.wait_ge(s["op2_psum"], i + 1)
                xs = X[:, t, n * 512:(n + 1) * 512]
                dve.tensor_tensor(xs, xs, PS[:, i % 4, :], ALU.add).then_inc(s["xo2_done"], 1)

            for t in range(NT + 1):
                if t < NT:
                    dve.wait_ge(s["rstat"], t + 1)
                    refine(rstd[:, t:t + 1], stat[:, t:t + 1], 1.0 / D)
                    dve.tensor_scalar(H2N[:, t, :], X[:, t, :], rstd[:, t:t + 1], None, ALU.mult).then_inc(s["h2_ready"], 1)
                if t >= 1:
                    dve.wait_ge(s["h2T_psum"], t)
                    if t >= 2:
                        dve.wait_ge(s["lg_psum"], t - 1)
                    for f in range(2):
                        i = dve.tensor_tensor(H2T[:, 4 * f:4 * f + 4, :], PS[:, 4 + 2 * ((t - 1) % 2) + f, :].rearrange("p (k c) -> p k c", k=4),
                                              bc(prm_c("n2g", 4 * f, 4), P), ALU.mult)
                    i.then_inc(s["h2T_ready"], 1)
            dve.wait_ge(s["lg_psum"], NT)
            lg = PS[:, 0, 0:NT * E].rearrange("p (t e) -> p t e", t=NT)
            own(dve.tensor_reduce(A4, lg, AX.X, ALU.max))
            own.settle()
            dve.tensor_tensor(AEX, lg, bc(A4, E), ALU.subtract).then_inc(s["lg_sub"], 1)
            dve.wait_ge(s["lg_exp"], 1)
            own(dve.tensor_reduce(A4B, AEX, AX.X, ALU.add))
            own.settle()
            own(dve.reciprocal(A4B, A4B))
            own.settle()
            dve.tensor_tensor(AFF, AEX, bc(A4B, E), ALU.mult).then_inc(s["aff_ready"], 1)
            dve.wait_ge(s["affT_psum"], 1)
            wk = AFFT[0:E, :]
            own(dve.tensor_copy(wk, PS[0:E, 1, :]))
            own.settle()
            for r in range(CAP // 8):
                v8 = VAL[0:E, 8 * r:8 * r + 8]
                own(dve.max(v8, wk))
                own.settle()
                own(dve.max_index(IDU[0:E, 8 * r:8 * r + 8], v8, wk))
                own.settle()
                if r < CAP // 8 - 1:
                    own(dve.match_replace(wk, v8, wk, -1.0))
                    own.settle()
            for f in range(2):
                own(dve.tensor_copy(IDF[0:E, f * CAP:(f + 1) * CAP], IDU[0:E, :]))
            dve.tensor_copy(VAL[0:E, CAP:2 * CAP], VAL[0:E, 0:CAP]).then_inc(s["tk_ready"], 1)
            dve.wait_ge(s["tkT_psum"], 1)
            dve.wait_ge(s["tab_in"], 80)
            own(dve.tensor_copy(IDT, PS[:, 2, 0:E]))
            own(dve.tensor_copy(GT, PS[:, 2, E:2 * E]))
            own(dve.tensor_copy(IDXB, PF[:, 3 * 512:5 * 512]))
            own.settle()

            def select(e):
                col = bass.ds(e * CAP, CAP)
                for t in range(NT):
                    i = dve.tensor_scalar(SEL[:, t, :], IDXB[:, col], iota_tok[:, t:t + 1], None, ALU.is_equal)
                i.then_inc(s["sel_ready"], 1)

            def gather_out(e):
                dve.wait_ge(s["gx_psum"], e + 1)
                dve.tensor_tensor(XE, PS[:, 7, :].rearrange("p (k c) -> p k c", k=KD), bc(prm_c("n2g", 0, 8), CAP), ALU.mult).then_inc(s["xe_ready"], 1)

            def expert(e, select_more, last_one):
                dve.wait_ge(s["s1_done"], e + 1)
                dve.wait_ge(s["w13_used"], (e + 1) * (2 * KD))
                dve.tensor_tensor(HH, S1, PF[:, 3 * 512:3 * 512 + FH], ALU.mult).then_inc(s["hh_done"], 1)
                dve.tensor_scalar(G, iota_row, IDT[:, bass.ds(e, 1)], GT[:, bass.ds(e, 1)], ALU.is_equal, ALU.mult).then_inc(s["gates_ready"], 1)
                if not last_one:
                    gather_out(e + 1)
                dve.wait_ge(s["ht_psum"], e + 1)
                dve.tensor_copy(HT[:, 4:FJ, :], PF[:, 4 * P:FH].rearrange("p (j c) -> p j c", c=P)).then_inc(s["ht_evD"], 1)
                if select_more:
                    dve.wait_ge(s["xe_ready"], e + 2)
                    select(e + 2)
                dve.wait_ge(s["w2_used"], (e + 1) * (2 * N2))
                dve.tensor_copy(YE, PS[:, 6, :]).then_inc(s["ye_ready"], 1)
                for n in range(2 * NT):
                    t, d = n // 2, n % 2
                    dve.wait_ge(s["sc_psum"], e * (2 * NT) + n + 1)
                    xs = X[:, t, d * 512:(d + 1) * 512]
                    dve.tensor_tensor(xs, xs, PS[:, [3, 4, 5, 7][n % 4], :], ALU.add).then_inc(s["sc_add"], 1)

            select(0)
            gather_out(0)
            select(1)
            with dve.Fori(0, E - 2) as e:
                expert(e, True, False)
            expert(E - 2, False, False)
            expert(E - 1, False, True)

        @block.tensor
        def _(pe):
            def project(dst, lhs, rhs, inc=None, v=None):
                for k in range(KD):
                    i = pe.matmul(dst, lhs(k), rhs(k), start=k == 0, stop=k == KD - 1)
                if inc:
                    i.then_inc(s[inc], 1)
                return i

            pe.wait_ge(s["cst_in"], 32)
            for t in range(5):
                _, n = toks(t)
                pe.wait_ge(s["u_ready"], t + 1)
                if t >= 2:
                    pe.wait_ge(s["ut_ready"], t - 1)
                for k in range(KD):
                    i = pe.transpose(PS[:, 2 * (t % 2) + k // 4, (k % 4) * P:(k % 4) * P + n], U[t % 2][0:n, k * P:(k + 1) * P], ident[0:n, 0:n])
                i.then_inc(s["ut_psum"], 1)
            pe.wait_ge(s["ut_ready"], 5)
            pe.wait_ge(ws_in[0], ws_level[0])
            w = group(0)
            for b in range(3):
                project(PS[:, 4 + b, :], lambda k: w[:, k, b * P:(b + 1) * P], lambda k: UT[:, k, 0:S], "lat_psum")
            project(PS[:, 7, 0:META], lambda k: w[:, k, 2 * P:3 * P], lambda k: UT[:, k, S:LT], "lat_psum")
            pe.wait_ge(ws_in[1], ws_level[1])
            w1g = group(1)
            for t in range(5):
                c, n = toks(t)
                i = project(PS[0:n, 2, 32 * t:32 * t + 32], lambda k: UT[:, k, c:c + n], lambda k: w1g[:, k, 0:32])
            i.then_inc(s["kr_psum"], 1)
            pe.wait_ge(s["sq_ready"], 4)
            pe.wait_ge(s["lat_ready"], 4)
            pe.wait_ge(s["gp_init"], 1)
            for t in range(NT):
                for b in range(2):
                    pe.matmul(PS[:, 7, 32 + t:33 + t], SQ[:, b * 512 + t * P:b * 512 + (t + 1) * P], ones, start=b == 0, stop=b == 1)
            for t in range(5):
                c, n = toks(t)
                i = pe.matmul(PS[0:n, 7, 36 + t:37 + t], SQ[:, 1024 + c:1024 + c + n], ones, start=True, stop=True)
            i.then_inc(s["stat_psum"], 1)
            for t in range(NT):
                if t >= 2:
                    pe.wait_ge(s["mz_free"], t - 1)
                project(PS[:, t % 2, :], lambda k: UT[:, k, t * P:(t + 1) * P], lambda k: w1g[:, k, 32:544], "mz_psum")
            pe.wait_ge(s["tab_in"], 80)

            def up(t):
                c, n = toks(t)
                if t >= 1:
                    pe.wait_ge(s["qk_evac"], t)
                if t < NT:
                    for f in range(2):
                        for b in range(2):
                            pe.matmul(PS[:, 3 + f, 0:384], CQT[:, b * S + c:b * S + c + P], UPW[:, b * 768 + f * 384:b * 768 + (f + 1) * 384],
                                      start=b == 0, stop=b == 1)
                for f in range(2):
                    i = pe.matmul(PS[0:n, 5 + f, :], CKVT[:, c:c + n], UPW[:, 1536 + f * 512:1536 + (f + 1) * 512], start=True, stop=True)
                i.then_inc(s["qk_psum"], 1)

            def turn_q(t):
                pe.wait_ge(s["q_ready"], t + 1)
                pe.wait_ge(s["rrT_evac"], t) if t >= 1 else pe.wait_ge(s["mz_free"], 4)
                for h in range(MH):
                    i = pe.transpose(PS[0:QH, h // 4, (h % 4) * P:(h % 4 + 1) * P], QTOK[t % 2][:, h * QH:(h + 1) * QH], ident)
                i.then_inc(s["qT_psum"], 1)

            def turn_k(t):
                c, n = toks(t)
                pe.wait_ge(s["k_ready"], t + 1)
                pe.wait_ge(s["qT_evac"], t + 1) if t < NT else pe.wait_ge(s["rrT_evac"], NT)
                for h in range(MH):
                    i = pe.transpose(PS[0:QH, h // 4, (h % 4) * P:(h % 4) * P + n], KTOK[t % 2][0:n, h * QH:(h + 1) * QH], ident[0:n, 0:n])
                i.then_inc(s["kT_psum"], 1)

            def ret_in(i):
                t = i % 5
                c, n = toks(t)
                g = 2 + i // 5
                if t == 0:
                    pe.wait_ge(ws_in[g % 2], ws_level[g])
                if i >= 2:
                    pe.wait_ge(s["e_free"], i - 1)
                elif i == 0:
                    pe.wait_ge(s["kr_copied"], 1)
                else:
                    pe.wait_ge(s["lat_rstd"], 1)
                b = [2, 7][i % 2]
                wg = group(g)
                if t < NT:
                    project(PS[:, b, :], lambda k: UT[:, k, c:c + n], lambda k: wg[:, k, :], "e_psum")
                elif i == 4:
                    project(PS[0:n, b, 256:512], lambda k: UT[:, k, c:c + n], lambda k: wg[:, k, 256:512], "e_psum")
                else:
                    project(PS[0:n, b, 0:256], lambda k: UT[:, k, c:c + n], lambda k: wg[:, k, 0:256], "e_psum")

            def turn_ret(t):
                c, n = toks(t)
                pe.wait_ge(s["rr_ready"], t + 1)
                pe.wait_ge(s["kT_evac"], t + 1)
                for j in range(0 if t < NT else 2, 4):
                    i = pe.transpose(PS[:, 0, j * P:j * P + n], RT1[0:n, j * P:(j + 1) * P], ident[0:n, 0:n])
                i.then_inc(s["rrT_psum"], 1)

            up(0), up(1), ret_in(0), turn_q(0), up(2), turn_k(0), ret_in(1), turn_ret(0), turn_q(1), up(3), turn_k(1)
            ret_in(2), turn_ret(1), turn_q(2), up(4), turn_k(2), ret_in(3), turn_ret(2), turn_q(3), ret_in(4), turn_k(3)
            turn_ret(3), ret_in(5), turn_k(4), ret_in(6), turn_ret(4)
            for i in range(7, 10):
                ret_in(i)
            pe.wait_ge(s["qk_evac"], 5)
            pe.wait_ge(s["e_free"], 9)
            pe.wait_ge(s["rrT_evac"], 5)
            pe.wait_ge(s["kT_evac"], 5)
            for n in range(8):
                g = 4 + n // 4
                if n % 4 == 0:
                    pe.wait_ge(ws_in[g % 2], ws_level[g])
                if n >= 4:
                    pe.wait_ge(s["cc_evac"] if n % 2 == 0 else s["cx_done"], (n - 4) // 2 + 1)
                wg = group(g)
                blk = (n % 2) * 256 + ((n % 4) // 2) * P
                if n < 4:
                    if n == 3:
                        pe.wait_ge(s["e_free"], 10)
                    project(PS[:, [0, 1, 2, 7][n], 0:2], lambda k: wg[:, k, blk:blk + P], lambda k: UT[:, k, LT - 2:LT])
                project(PS[:, 3 + n % 4, :], lambda k: wg[:, k, blk:blk + P], lambda k: UT[:, k, 0:S], "f_psum")

            def ret_scores(h):
                j, o = h // 2, 64 * (h % 2)
                for b in range(5):
                    i = 5 * h + b
                    if i >= 4:
                        pe.wait_ge(s["ret_s"], i - 3)
                    c, n = toks(b)
                    q0 = c if b < NT else 0
                    pe.matmul(PS[0:n, i % 4, 0:S - q0], RKT[o:o + 64, j, c:c + n], RQT[o:o + 64, j, q0:S], start=True, stop=True)\
                        .then_inc(s["rs_psum"], 1)

            def ret_out(h):
                pe.wait_ge(s["ret_s"], 5 * h + 5)
                sd = SD[h % 2]
                for t in range(NT):
                    dst = PS[:, 6 + t // 2, (t % 2) * 256 + h * 64:(t % 2) * 256 + h * 64 + 64]
                    for b in range(t + 1):
                        o = [0, 512, 896, 1152][b] + (t - b) * P
                        pe.matmul(dst, sd[:, o:o + P], RV[:, b * 256 + h * 64:b * 256 + h * 64 + 64], start=b == 0, stop=False)
                    i = pe.matmul(dst, sd[0:META, 1280 + t * P:1280 + (t + 1) * P], RV[0:META, 1024 + h * 64:1088 + h * 64], start=False, stop=True)
                i.then_inc(s["ro_psum"], 1)

            pe.wait_ge(s["cc_evac"], 2)
            pe.wait_ge(s["cx_done"], 2)
            pe.wait_ge(s["cz_exp"], 1)
            pe.wait_ge(s["cz_done"], 1)
            ret_scores(0)
            for h in range(RH):
                if h + 1 < RH:
                    ret_scores(h + 1)
                ret_out(h)

            def scores(i):
                t, h, b = i // MH, i % MH, 2 * (i % 2)
                n = (t + 1) * P
                if i >= 2:
                    pe.wait_ge(s["p_done"], i - 1)
                q = QT[0:QH, h, t * P:(t + 1) * P]
                pe.matmul(PS[:, b, 0:n - 64], q, KT[0:QH, h, 0:n - 64], start=True, stop=True)
                pe.matmul(PS[:, b, n - 64:n], q, KT[0:QH, h, n - 64:n], start=True, stop=False)
                pe.matmul(PS[:, b, n - 64:n], rmask[0:1, :], nrow[0:1, :], start=False, stop=True)
                a = b * 512 + n
                pe.matmul(PF[:, a:a + META], q, KT[0:QH, h, S:LT], start=True, stop=True).then_inc(s["s_psum"], 1)

            def turn_p(i):
                t = i // MH
                pe.wait_ge(s["p_done"], i + 1)
                if i >= 2:
                    pe.wait_ge(s["pt_evac"], i - 1)
                for b in range(t + 1):
                    pe.transpose(PS[:, 4 + i % 2, b * P:(b + 1) * P], PB[i % 2][:, b * P:(b + 1) * P], ident)
                if t == NT - 1:
                    pe.wait_ge(s["pt_evac"], i)
                    pe.wait_ge(s["yo_free"], NT - 1)
                pe.transpose(meta_pt(i), PB[i % 2][:, (t + 1) * P:(t + 1) * P + META], ident).then_inc(s["pt_psum"], 1)

            def values(i):
                t, h = i // MH, i % MH
                pe.wait_ge(s["pt_evac"], i + 1)
                if h == 0 and t >= 2:
                    pe.wait_ge(s["yo_free"], t - 1)
                if i == 0:
                    pe.wait_ge(s["yr_ready"], 1)
                dst = PS[:, 6 + t % 2, h * VH:(h + 1) * VH]
                for b in range(t + 1):
                    pe.matmul(dst, PTS[i % 2][:, b * P:(b + 1) * P], V1[:, b * 512 + h * VH:b * 512 + (h + 1) * VH], start=b == 0, stop=False)
                pe.matmul(dst, PTS[i % 2][0:META, 512:640], V1[0:META, NT * 512 + h * VH:NT * 512 + (h + 1) * VH], start=False, stop=True)\
                    .then_inc(s["pv_psum"], 1)

            def turn_y(t):
                pe.wait_ge(s["ym_ready"], t + 1)
                if t >= 1:
                    pe.wait_ge(s["yt_evac"], min(t, NT - 2))
                for j in range(4):
                    i = pe.transpose(PS[:, 3 if t == 3 else 1, j * P:(j + 1) * P], YM[t % 2][:, j * P:(j + 1) * P], ident)
                i.then_inc(s["yt_psum"], 1)

            pe.wait_ge(s["ret_s"], 5 * RH)
            scores(0), scores(1)
            for i in range(NT * MH):
                turn_p(i)
                if i == 1:
                    pe.wait_ge(s["yr_ready"], 1)
                    for t in range(NT):
                        for j in range(2):
                            ins = pe.transpose(PS[:, 1 + 2 * j, t * P:(t + 1) * P], YR[:, t * 256 + j * P:t * 256 + (j + 1) * P], ident)
                    ins.then_inc(s["yrT_psum"], 1)
                if i + 2 < NT * MH:
                    scores(i + 2)
                values(i)
                if i in (MH + 2, 2 * MH + 2):
                    if i // MH == 1:
                        pe.wait_ge(s["yrT_evac"], 1)
                    turn_y(i // MH - 1)
            turn_y(NT - 2)
            turn_y(NT - 1)

            pe.wait_ge(s["yt_evac"], NT)
            pe.wait_ge(s["yrT_evac"], 1)
            pe.wait_ge(s["conv_y"], 2)
            for i in range(2 * NT):
                n, t = i // NT, i % NT
                if t == 0:
                    pe.wait_ge(ws_in[(6 + n) % 2], ws_level[6 + n])
                if i >= 4:
                    pe.wait_ge(s["xo_done"], i - 3)
                wg = group(6 + n)
                project(PS[:, i % 4, :], lambda k: YT[:, k, t * P:(t + 1) * P], lambda k: wg[:, k, :], "op_psum")
            for t in range(NT):
                pe.wait_ge(s["u2_ready"], t + 1)
                if t >= 2:
                    pe.wait_ge(s["ut2_ready"], t - 1)
                for k in range(KD):
                    i = pe.transpose(PS[:, 4 + 2 * (t % 2) + k // 4, (k % 4) * P:(k % 4 + 1) * P], U2[t % 2][:, k * P:(k + 1) * P], ident)
                i.then_inc(s["ut2_psum"], 1)
            pe.wait_ge(s["ut2_ready"], NT)
            pe.wait_ge(s["xo_done"], 2 * NT)
            for j in range(4):
                g = 8 + j // 2
                if j % 2 == 0:
                    pe.wait_ge(ws_in[g % 2], ws_level[g])
                if j >= 2:
                    pe.wait_ge(s["cu_done"], j - 1)
                wg = group(g)
                for f in range(2):
                    blk = f * 256 + (j % 2) * P
                    project(PS[:, (2 * j + f) % 4, :], lambda k: wg[:, k, blk:blk + P], lambda k: UT2[:, k, :], "f2_psum")

            def turn_z(i):
                pe.wait_ge(s["zr_ready"], i + 1)
                if i >= 2:
                    pe.wait_ge(s["zT_evac"], i - 1)
                else:
                    pe.wait_ge(s["cu_done"], 4)
                for j in range(4):
                    ins = pe.transpose(PS[:, i % 2, j * P:(j + 1) * P], XT1[:, j * P:(j + 1) * P], ident)
                ins.then_inc(s["zT_psum"], 1)

            for i in range(3 * NT):
                g, t = 10 + i // NT, i % NT
                if t == 0:
                    pe.wait_ge(ws_in[g % 2], ws_level[g])
                if i >= 4:
                    pe.wait_ge(s["z_free"], i - 3)
                wg = group(g)
                project(PS[:, 4 + i % 4, :], lambda k: UT2[:, k, t * P:(t + 1) * P], lambda k: wg[:, k, :], "z_psum")
                if 1 <= i <= 2 * NT:
                    turn_z(i - 1)

            def scores2(i):
                t, h = i // H2, i % H2
                if i >= 2:
                    pe.wait_ge(s["nm2_ready"], i - 1)
                j, o = h // 2, 64 * (h % 2)
                pe.matmul(PS[:, i % 2, :], QT2[o:o + 64, j, t * P:(t + 1) * P], KT2[o:o + 64, j, :], start=True, stop=True).then_inc(s["s2_psum"], 1)

            def turn_p2(i):
                pe.wait_ge(s["p2_done"], i + 1)
                if i >= 2:
                    pe.wait_ge(s["pt2_evA"], i - 1)
                for b in range(4):
                    ins = pe.transpose(PS[:, 2 + i % 2, b * P:(b + 1) * P], SM[i % 2][:, b * P:(b + 1) * P], ident)
                ins.then_inc(s["pt2_psum"], 1)

            def values2(i):
                t, h = i // H2, i % H2
                pe.wait_ge(s["pt2_evA"], i + 1)
                if h == 0 and t >= 2:
                    pe.wait_ge(s["ym2_ready"], t - 1)
                for b in range(NT):
                    ins = pe.matmul(PS[:, 4 + t % 2, h * HD:(h + 1) * HD], PT2[i % 2][:, b * P:(b + 1) * P],
                                    V2[:, b * 512 + h * HD:b * 512 + (h + 1) * HD], start=b == 0, stop=b == NT - 1)
                ins.then_inc(s["pv2_psum"], 1)

            def turn_y2(t):
                pe.wait_ge(s["ym2_ready"], t + 1)
                if t >= 1:
                    pe.wait_ge(s["yt2_evac"], t)
                for j in range(4):
                    i = pe.transpose(PS[:, 6, j * P:(j + 1) * P], YM2[t % 2][:, j * P:(j + 1) * P], ident)
                i.then_inc(s["yt2_psum"], 1)

            pe.wait_ge(s["zT_evac"], 2 * NT)
            pe.wait_ge(s["v_evac"], NT)
            scores2(0), scores2(1)
            for i in range(NT * H2):
                turn_p2(i)
                if i + 2 < NT * H2:
                    scores2(i + 2)
                values2(i)
                if i % H2 == 2 and i > H2:
                    turn_y2(i // H2 - 1)
                if i == LN_AT:
                    pe.wait_ge(s["cv_done"], 1)
                    for j in range(4):
                        ins = pe.matmul(PS[:, 7, :], LN_ONES, CA[:, j, :], start=j == 0, stop=j == 3)
                    ins.then_inc(s["mean_psum"], 1)
                if i == LN_AT + 2:
                    pe.wait_ge(s["cen_done"], 4)
                    pe.wait_ge(s["lsq_done"], 4)
                    for j in range(4):
                        ins = pe.matmul(PS[:, 7, :], LN_ONES, LSQ[:, j, :], start=j == 0, stop=j == 3)
                    ins.then_inc(s["var_psum"], 1)
            turn_y2(NT - 1)
            pe.wait_ge(s["yt2_evac"], NT)
            pe.wait_ge(s["y2_done"], 4)
            for i in range(2 * NT):
                n, t = i // NT, i % NT
                if t == 0:
                    pe.wait_ge(ws_in[(13 + n) % 2], ws_level[13 + n])
                if i >= 4:
                    pe.wait_ge(s["xo2_done"], i - 3)
                wg = group(13 + n)
                project(PS[:, i % 4, :], lambda k: YT2[:, k, t * P:(t + 1) * P], lambda k: wg[:, k, :], "op2_psum")

            pe.wait_ge(s["tab_in"], 80)
            pe.wait_ge(s["lv_ready"], 1)

            def logits(t):
                pe.wait_ge(s["h2T_ready"], t + 1)
                for k in range(KD):
                    i = pe.matmul(PS[:, 0, t * E:(t + 1) * E], H2T[:, k, :], wr[:, k, :], start=k == 0, stop=k == KD - 1)
                i.then_inc(s["lg_psum"], 1)

            for t in range(NT):
                pe.wait_ge(s["h2_ready"], t + 1)
                if t >= 2:
                    pe.wait_ge(s["h2T_ready"], t - 1)
                for k in range(KD):
                    i = pe.transpose(PS[:, 4 + 2 * (t % 2) + k // 4, (k % 4) * P:(k % 4 + 1) * P], H2N[:, t, k * P:(k + 1) * P], ident)
                i.then_inc(s["h2T_psum"], 1)
                if t == 0:
                    pe.wait_ge(s["xo2_done"], 2 * NT)
                if t >= 1:
                    logits(t - 1)
            logits(NT - 1)
            pe.wait_ge(s["aff_ready"], 1)
            for t in range(NT):
                i = pe.transpose(PS[0:E, 1, t * P:(t + 1) * P], AFF[:, t, :], ident)
            i.then_inc(s["affT_psum"], 1)
            pe.wait_ge(s["tk_ready"], 1)
            pe.transpose(PS[:, 2, 0:E], IDF[0:E, :], ident[0:E, 0:E])
            pe.transpose(PS[:, 2, E:2 * E], VAL[0:E, :], ident[0:E, 0:E])
            for e in range(E):
                i = pe.matmul(PF[:, 3 * 512 + e * CAP:3 * 512 + (e + 1) * CAP], ident[0:E, e:e + 1].to_broadcast([E, P]), IDF[0:E, 0:CAP],
                              start=True, stop=True)
            i.then_inc(s["tkT_psum"], 1)

            def gather(e):
                pe.wait_ge(s["sel_ready"], e + 1)
                for k in range(KD):
                    for t in range(NT):
                        i = pe.matmul(PS[:, 7, k * CAP:(k + 1) * CAP], H2N[:, t, k * P:(k + 1) * P], SEL[:, t, :], start=t == 0, stop=t == NT - 1)
                i.then_inc(s["gx_psum"], 1)

            def up13(e, third):
                bank = 3 if third else 0
                for k in range(KD):
                    pe.wait_ge(w13_in[k], (2 * e + (2 if third else 1)) * 16)
                    for c, n in FCH:
                        for f in range(2):
                            i = pe.matmul(PS[64 * f:64 * f + 64, bank + c // 512, 0:n], XE[:, k, :], W13[k][:, f * FH + c:f * FH + c + n],
                                          start=k == 0, stop=k == KD - 1, skip_group_check=True)
                    i.then_inc(s["w13_used"], 1)

            def expert(e, first, last_one):
                pe.wait_ge(s["xe_ready"], e + 1)
                if not first:
                    pe.wait_ge(s["ht_evD"], e)
                    pe.wait_ge(s["ht_evA"], e)
                up13(e, False)
                if not first:
                    pe.wait_ge(s["sc_add"], e * (2 * NT))
                up13(e, True)
                if not last_one:
                    gather(e + 1)
                pe.wait_ge(s["hh_done"], e + 1)
                for j in range(FJ):
                    i = pe.transpose(PF[:, j * P:(j + 1) * P], HH[:, j * P:(j + 1) * P], ident)
                i.then_inc(s["ht_psum"], 1)
                pe.wait_ge(s["ht_evA"], e + 1)
                pe.wait_ge(s["ht_evD"], e + 1)
                for i in range(2 * FJ):
                    j, f = i // 2, i % 2
                    pe.wait_ge(w2_in[i % N2], (2 * e + i // N2 + 1) * 16)
                    for d in range(2):
                        ins = pe.matmul(PS[64 * d:64 * d + 64, 6, :], HT[:, j, 64 * f:64 * f + 64], W2S[i % N2][:, d * 512:(d + 1) * 512],
                                        start=i == 0, stop=i == 2 * FJ - 1, skip_group_check=True)
                    ins.then_inc(s["w2_used"], 1)
                pe.wait_ge(s["ye_ready"], e + 1)
                pe.wait_ge(s["gates_ready"], e + 1)
                if not last_one:
                    pe.wait_ge(s["xe_ready"], e + 2)
                for n in range(2 * NT):
                    t, d = n // 2, n % 2
                    if n >= 4:
                        pe.wait_ge(s["sc_add"], e * (2 * NT) + n - 3)
                    pe.matmul(PS[:, [3, 4, 5, 7][n % 4], :], G[64 * d:64 * d + 64, t * P:(t + 1) * P], YE[64 * d:64 * d + 64, :],
                              start=True, stop=True).then_inc(s["sc_psum"], 1)

            gather(0)
            expert(0, True, False)
            with pe.Fori(1, E - 1) as e:
                expert(e, False, False)
            expert(E - 1, False, True)


LN_AT = 14
TAPS_PER_TILE = 11
TAPS_PER_HEAD = 4


def _tables():
    f = np.float32

    def ropes(dim, pos):
        inv = (f(1.0) / (f(10000.0) ** (np.arange(0, dim, 2, dtype=f) / f(dim)))).astype(f)
        ang = (pos.astype(f)[..., None] * inv).astype(np.float64)
        c, sn = np.cos(ang), np.sin(ang)
        return np.concatenate([c, c], -1), np.concatenate([-sn, sn], -1)

    p = np.arange(P)
    pos1 = np.stack([META + t * P + p for t in range(NT)] + [p], 1)
    pos2 = np.stack([t * P + p for t in range(NT)], 1)
    tab = np.zeros((P, NTAB), f)

    def put(name, v):
        a, n = TAB[name]
        tab[:, a:a + n] = v.reshape(P, n)

    for names, dim, pos in ((("mcc", "mss"), ROPE, pos1), (("rcc", "rss"), RD, pos1), (("bcc", "bss"), HD, pos2)):
        for name, v in zip(names, ropes(dim, pos)):
            put(name, v)
    c = np.arange(LT)
    lg = np.log1p(-np.exp2(-5.0 - np.arange(RH)))
    d = np.exp(lg[None, :, None] * np.abs(c[None, None, :] - p[:, None, None])) * RD ** -0.5
    put("dec", np.where((p[:, None] // 64 <= c[None, :] // 64)[:, None, :], d, 0.0))
    y = np.arange(2 * S - P)
    dist = np.abs(p[:, None] - (y[None, :] - (S - P)))
    n = (dist <= 64) * 1 + ((dist % 4 == 0) & (dist <= 256)) + ((dist % 16 == 0) & (dist <= 1024))
    put("cm", np.where(n > 0, np.log(np.maximum(n, 1)), NEG))
    iota = np.concatenate([np.broadcast_to(np.arange(S, dtype=f), (P, S)), pos2.astype(f)], 1)
    return tab, iota


def kernel(**inputs):
    import concourse.bacc as bacc
    from concourse.bass_utils import run_bass_kernel_spmd

    v = {k: np.asarray(a) for k, a in inputs.items()}
    f = np.float32
    prm = np.ones((P, NPRM), f)

    def put(name, a):
        at, n = PRM[name]
        prm[:a.shape[0], at:at + n] = a.reshape(a.shape[0], n)

    def cols(a):
        return a.reshape(-1, P).T

    def rep(a):
        return np.broadcast_to(a, (P, a.shape[0]))

    def swap(a):
        h = a.shape[0] // 2
        return np.concatenate([a[h:], a[:h]])

    put("lnw", cols(v["ln_w"][0]))
    put("qan", cols(v["q_a_norm"][0]))
    put("kvan", cols(v["kv_a_norm"][0]))
    put("qn", v["q_norm"][0][:NOPE, None])
    put("kn", v["k_norm"][0][:NOPE, None])
    put("cw", v["conv_w"][0].reshape(3, 2, P).transpose(2, 1, 0))
    put("cb", cols(v["conv_b"][0]))
    put("n1g", cols(v["norm1_g_2"]))
    put("dw", v["conv_dw_w_2"].reshape(TAPS, 4, P).transpose(2, 1, 0))
    put("dwb", cols(v["conv_dw_b_2"]))
    put("lng", cols(v["conv_ln_g_2"]))
    put("lnb", cols(v["conv_ln_b_2"]))
    put("n2g", cols(v["norm2_g_2"]))
    for a, b, w in (("qr", "qrs", v["q_norm"][0][NOPE:]), ("kr", "krs", v["k_norm"][0][NOPE:]),
                    ("q2", "q2s", v["q_norm_g_2"]), ("k2", "k2s", v["k_norm_g_2"])):
        put(a, rep(w))
        put(b, rep(swap(w)))
    put("retn", rep(v["ret_norm"][0]))
    tab, iota = _tables()
    arrays = {
        "x": v["x"][0], "meta": v["meta_tokens"], "w_in": v["w_in"][0], "w_out": v["w_out"][0], "w_in_2": v["w_in_2"],
        "w_out_2": v["w_out_2"], "w_uq": v["w_uq"][0], "w_ukv": v["w_ukv"][0], "w_router": v["w_router_2"],
        "w1": v["w1_2"], "w3": v["w3_2"], "w2": v["w2_2"], "prm": prm, "ident": np.eye(P, dtype=f), "tab": tab, "iota": iota,
    }
    arrays = {f"in_{k}": np.ascontiguousarray(a) for k, a in arrays.items()}
    nc = bacc.Bacc("TRN2", target_bir_lowering=False, num_devices=1)
    d = {k[3:]: nc.dram_tensor(k, a.shape, mybir.dt.from_np(a.dtype), kind="ExternalInput").ap() for k, a in arrays.items()}
    out = nc.dram_tensor("out_x", (S, D), F32, kind="ExternalOutput").ap()
    build(nc, d["x"], d["meta"], {k: d[k] for k in ("w_in", "w_out", "w_in_2", "w_out_2")}, d["w_uq"], d["w_ukv"], d["w_router"],
          d["w1"], d["w3"], d["w2"], d["prm"], d["ident"], d["tab"], d["iota"], out)
    r = run_bass_kernel_spmd(nc, [arrays], core_ids=[0])
    return r.results[0]["out_x"].reshape(1, S, D)
```

```python
from contextlib import ExitStack

import numpy as np

import concourse.bass as bass
from concourse import mybir

F32 = mybir.dt.float32
U32 = mybir.dt.uint32
ALU = mybir.AluOpType
ACT = mybir.ActivationFunctionType
AX = mybir.AxisListType

P = 128
D = 1024
KD = D // P
S = 512
NT = S // P
META = 16
LT = S + META
EPS = 1e-6
NEG = -1.0e30
QH, NOPE, ROPE, VH, MH = 96, 64, 32, 64, 8
RH, RD = 4, 64
C_CX, C_CB, C_CC, C_CZ, C_Q, C_KR, C_RQ, C_RV = 0, 256, 512, 768, 1024, 1408, 1952, 2464
H2, HD = 8, 64
TAPS, PAD = 31, 15
CW = S + 2 * PAD
E, CAP, FF = 16, 64, 2816
FH = FF // 2
FJ = FH // P
FCH = [(0, 512), (512, 512), (1024, 384)]

TOTAL = 53200
R13, R2 = 0, KD * FF
N2 = 11
WS = R2 + N2 * D
WSLOT = KD * 544
XOFF = WS + 2 * WSLOT
SMALL = XOFF + NT * D

PRM = {}


def _prm_layout():
    at = 0
    for name, n in (("lnw", 8), ("qan", 2), ("kvan", 1), ("qn", 1), ("kn", 1), ("cw", 6), ("cb", 2), ("n1g", 8),
                    ("dw", 4 * TAPS), ("dwb", 4), ("lng", 4), ("lnb", 4), ("n2g", 8),
                    ("qr", 32), ("qrs", 32), ("kr", 32), ("krs", 32), ("retc", 1),
                    ("q2", 64), ("q2s", 64), ("k2", 64), ("k2s", 64)):
        PRM[name] = (at, n)
        at += n
    return at


NPRM = _prm_layout()
TAB = {}


def _tab_layout():
    at = 0
    for name, n in (("mcc", 5 * 32), ("mss", 5 * 32), ("rcc", 5 * 64), ("rss", 5 * 64), ("bcc", 4 * 64), ("bss", 4 * 64),
                    ("dec", RH * LT), ("cm", 2 * S - P), ("rones", P)):
        TAB[name] = (at, n)
        at += n
    return at


NTAB = _tab_layout()
GROUPS = [("w_in", [(C_Q, 384)]), ("w_in", [(C_KR, 544)]), ("w_in", [(C_RQ, 512)]), ("w_in", [(C_RV, 512)]),
          ("w_in", [(C_CC, 256), (C_CX, 256)]), ("w_in", [(C_CZ, 256), (C_CB, 256)]),
          ("w_out", [(0, 512)]), ("w_out", [(512, 512)]),
          ("w_in_2", [(2048, 256), (1536, 256)]), ("w_in_2", [(2304, 256), (1792, 256)]),
          ("w_in_2", [(0, 512)]), ("w_in_2", [(512, 512)]), ("w_in_2", [(1024, 512)]),
          ("w_out_2", [(0, 512)]), ("w_out_2", [(512, 512)])]


class Carve:

    def __init__(self, arena, at, end):
        self.arena, self.at, self.end = arena, at, end

    def __call__(self, n):
        a = self.at
        self.at += n
        assert self.at <= self.end, (self.at, self.end)
        return self.arena[:, a:a + n]


class Own:

    def __init__(self, eng, sem):
        self.eng, self.sem, self.n = eng, sem, 0

    def __call__(self, ins):
        ins.then_inc(self.sem, 1)
        self.n += 1
        return self.n

    def settle(self, upto=None):
        self.eng.wait_ge(self.sem, self.n if upto is None else upto)


def build(nc, x, meta, wd, w_uq, w_ukv, w_router, w1, w3, w2, prm, ident_d, tab_d, iota_d, mask_d, out):
    with ExitStack() as ctx:
        A = ctx.enter_context(nc.sbuf_tensor("arena", [P, TOTAL], F32))
        PS = ctx.enter_context(nc.psum_tensor("PS", [P, 8, 512], F32))
        PF = PS[:, :, :].rearrange("p b c -> p (b c)")

        def sem(name):
            return ctx.enter_context(nc.semaphore(name))

        X = A[:, XOFF:XOFF + NT * D].rearrange("p (t d) -> p t d", t=NT)
        sm = Carve(A, SMALL, TOTAL)
        ident = sm(P)
        prm_s = sm(NPRM)
        wr = sm(KD * E).rearrange("p (k e) -> p k e", k=KD)
        iota = sm(S + NT)
        iota_row, iota_tok = iota[:, 0:S], iota[:, S:S + NT]
        ones = sm(1)
        eps = sm(1)
        stat = sm(9)
        rstd = sm(9)
        newt = sm(16)
        var = sm(16)
        ms = [sm(16), sm(16)]
        rs = [sm(16), sm(16)]
        nmax = sm(4)
        lsum = sm(32)
        krs = sm(5)
        linv = sm(32)
        TB = sm.at
        tab = sm(NTAB)

        def prm_c(name, i=0, n=1):
            a, _ = PRM[name]
            return prm_s[:, a + i:a + i + n]

        def tab_c(name):
            a, n = TAB[name]
            return tab[:, a:a + n]

        mcc, mss, rcc, rss = (tab_c(n).rearrange("p (t c) -> p t c", t=5) for n in ("mcc", "mss", "rcc", "rss"))
        bcc, bss = (tab_c(n).rearrange("p (t c) -> p t c", t=4) for n in ("bcc", "bss"))
        dec = tab_c("dec").rearrange("p (h c) -> p h c", h=RH)
        cm = tab_c("cm")
        ret_ones = tab_c("rones")

        c1 = Carve(A, 0, WS)
        UT = c1(KD * LT).rearrange("p (k c) -> p k c", k=KD)
        YT = A[:, 0:KD * S].rearrange("p (k c) -> p k c", k=KD)
        BUFA = c1(2400)
        U = [BUFA[:, 0:D], BUFA[:, D:2 * D]]
        SQ = BUFA[:, 0:1552]
        QSQ = BUFA[:, 0:1280]
        CQT = c1(2 * S)
        CKVT = c1(LT)
        MZ = c1(NT * 512)
        RQT = c1(2 * S).rearrange("p (j c) -> p j c", j=2)
        RKT = c1(2 * LT).rearrange("p (j c) -> p j c", j=2)
        RV = c1(5 * 256)
        UP0 = c1.at
        SRZ = c1(1024)
        XM = SRZ
        CU1 = c1(2 * (S + 2)).rearrange("p (b c) -> p b c", b=2)
        SD3 = A[:, c1.at - 2 * (S + 2):c1.at - 2 * (S + 2) + 1792]
        CG = c1(1028)[:, 0:1024].rearrange("p (b c) -> p b c", b=2)
        UPW = A[:, UP0:UP0 + 2 * 768 + 1024]
        CGF = CG.rearrange("p b c -> p (b c)")
        KR, KRQ, KRT = (CGF[:, 512 + 160 * i:672 + 160 * i].rearrange("p (t c) -> p t c", t=5) for i in range(3))
        QK0 = c1.at
        QTOK = [c1(768), c1(768)]
        KTOK = [c1(768), c1(768)]
        V1 = c1(5 * 512)
        QT = c1(MH * S).rearrange("p (h c) -> p h c", h=MH)
        KT = c1(MH * LT).rearrange("p (h c) -> p h c", h=MH)
        rq_a, rq_b = (c1(4 * 32).rearrange("p (t c) -> p t c", t=4) for _ in range(2))
        rk_a, rk_b = (c1(5 * 32).rearrange("p (t c) -> p t c", t=5) for _ in range(2))
        RT1, RT2 = c1(512), c1(512)
        SCR = c1(1024)
        SD = [A[:, QK0:QK0 + 1792], BUFA[:, 0:1792], A[:, c1.at - 2048:c1.at - 256], SD3]
        RSQ = [BUFA[:, 0:512], BUFA[:, 512:1024]]
        RVAR = [BUFA[:, 1024:1536], BUFA[:, 1536:2048]]
        RFAC = [A[:, QK0:QK0 + 512], A[:, QK0 + 512:QK0 + 1024]]
        RTMP = A[:, QK0 + 1024:QK0 + 1536]
        PB = [BUFA[:, LT * i:LT * (i + 1)] for i in range(4)] + [A[:, QK0 + LT * i:QK0 + LT * (i + 1)] for i in range(2)]
        PT = A[:, QK0 + 2 * LT:QK0 + 2 * LT + 1024].rearrange("p (f c) -> p f c", f=2)
        PTM = A[:, QK0 + 2 * LT + 1024:QK0 + 2 * LT + 1280].rearrange("p (f c) -> p f c", f=2)
        KRG = c1(160).rearrange("p (t c) -> p t c", t=5)

        c2 = Carve(A, KD * LT, R2 + (N2 - 4) * D)
        U2f = c2(2048)
        U2 = [U2f[:, 0:D], U2f[:, D:2 * D]]
        UT2 = c2(KD * S).rearrange("p (k c) -> p k c", k=KD)
        CU2 = c2(4 * CW).rearrange("p (b c) -> p b c", b=4)
        CA = c2(4 * S).rearrange("p (b c) -> p b c", b=4)
        SCB = [c2(512), c2(512)]
        LV, LY, LA = c2(512), c2(512), c2(512)
        XN, XT1, XT2, XSQ = c2(512), c2(512), c2(512), c2(512)
        V2 = c2(NT * 512)
        QT2, KT2 = (c2(4 * S).rearrange("p (j c) -> p j c", j=4) for _ in range(2))
        SM = [UT2.rearrange("p k c -> p (k c)")[:, 512 * i:512 * (i + 1)] for i in range(6)]
        PT2 = c2(1024).rearrange("p (f c) -> p f c", f=2)
        tq_a, tq_b, tk_a, tk_b = (c2(4 * 64).rearrange("p (t c) -> p t c", t=4) for _ in range(4))
        YT2 = A[:, R2 + (N2 - 4) * D:WS].rearrange("p (k c) -> p k c", k=KD)
        TAP = [YT2[:, k, :] for k in range(KD)]
        LN_ONES = c2(P)
        LSQ = U2f.rearrange("p (b c) -> p b c", b=4)

        W13 = [A[:, R13 + k * FF:R13 + (k + 1) * FF] for k in range(KD)]
        W2S = [A[:, R2 + i * D:R2 + (i + 1) * D] for i in range(N2)]
        H2N = A[:, WS + WSLOT:WS + WSLOT + NT * D].rearrange("p (t d) -> p t d", t=NT)
        ca = Carve(A, WS, WS + WSLOT)
        S1, HH = ca(FH), ca(FH)
        HT = ca(FJ * P).rearrange("p (j c) -> p j c", j=FJ)
        cb = Carve(A, TB, TOTAL)
        IDXB = cb(E * CAP)
        SEL = cb(NT * CAP).rearrange("p (t c) -> p t c", t=NT)
        cb_g = cb.at
        G = cb(S)
        XE = cb(KD * CAP).rearrange("p (k c) -> p k c", k=KD)
        YE = cb(512)
        H2T = cb(D).rearrange("p (k c) -> p k c", k=KD)
        AFFT = cb(S)
        AFF = A[:, WS:WS + 64].rearrange("p (t e) -> p t e", t=NT)
        AEX = A[:, WS + 64:WS + 128].rearrange("p (t e) -> p t e", t=NT)
        A4, A4B = A[:, WS + 128:WS + 132], A[:, WS + 132:WS + 136]
        VAL = A[:, WS + 136:WS + 264]
        IDU = A[:, WS + 264:WS + 328].bitcast(U32)
        IDF = A[:, WS + 328:WS + 456]
        GT, IDT = cb(E), cb(E)
        IDD = H2T.rearrange("p k c -> p (k c)")
        HR = [IDXB, A[:, cb_g:cb_g + D]]

        WSL = [A[:, WS + i * WSLOT:WS + (i + 1) * WSLOT] for i in range(2)]

        names = """cst_in tab_in gp_init gp_rope ustat u_ready ut_psum ut_ready lat_psum sq_ready lat_ready stat_psum lat_exp
        lat_rstd kr_psum kr_copied mz_psum mz_exp mz_free qk_psum qk_evac ms_ready ms_exp q_ready k_ready qT_psum
        kT_psum qT_evac kT_evac e_psum e_free rr_ready rrT_psum rrT_evac rz_exp f_psum cc_evac cx_done cz_exp cz_done
        conv_y rs_psum ret_s ro_psum ro_sq ro_ms ro_v ro_exp yr_ready rv_evac s_psum nm_ready p_done pt_psum
        pt_evac ptm_evac ps_ready pv_psum yo_free op_psum xo_done ustat2 u2_ready ut2_psum ut2_ready
        pads f2_psum b_exp cu_done z_psum z_sq z_ms z_rs z_free zr_ready zT_psum zT_evac v_evac s2_psum nm2_ready
        p2_done pt2_psum pt2_evA pv2_psum ps2_ready yt2_evac cv_done tap_ready tap_added mean_psum cen_done lsq_done
        var_psum lv_ready lrs_done ly_ready ly_exp y2_done op2_psum xo2_done rstat idd_ready h2n_ready h2_ready h2T_psum h2T_ready lg_psum
        lg_sub lg_exp aff_ready affT_psum tk_ready tkT_psum gates_ready sel_ready gx_psum xe_ready s1_done hh_done
        w13_used w2_used ht_psum ht_evD ht_evA ye_ready sc_psum sc_add out_done act_own dve_own gp_own""".split()
        s = {n: sem(n) for n in names}
        x_in = [sem(f"x_in{i}") for i in range(5)]
        ws_in = [sem(f"ws_in{i}") for i in range(2)]
        w13_in = [sem(f"w13_in{i}") for i in range(KD)]
        w2_in = [sem(f"w2_in{i}") for i in range(N2)]

        ws_level, level = [], [0, 0]
        for g, (_, parts) in enumerate(GROUPS):
            level[g % 2] += 16 * len(parts)
            ws_level.append(level[g % 2])
        released = {0: ("lat_psum", 4), 1: ("mz_psum", 4), 2: ("e_psum", 5), 3: ("e_psum", 12), 4: ("f_psum", 4),
                    5: ("f_psum", 8), 6: ("op_psum", 7), 7: ("op_psum", 8), 8: ("f2_psum", 4), 9: ("f2_psum", 8),
                    10: ("z_psum", 4), 11: ("z_psum", 8), 12: ("z_psum", 12)}

        def group(g):
            n = sum(c for _, c in GROUPS[g][1])
            return WSL[g % 2][:, 0:KD * n].rearrange("p (k c) -> p k c", k=KD)

        def score_bank(i):
            return i % 4 if i < (NT - 1) * MH else 2 * (i % 2)

        def toks(t):
            return (t * P, P) if t < NT else (S, META)

        block = ctx.enter_context(nc.Block())

        @block.sync
        def _(sp):
            def load_group(g):
                if g >= 2:
                    name, v = released[g - 2]
                    sp.wait_ge(s[name], v)
                at = 0
                for c, n in GROUPS[g][1]:
                    sp.dma_start(group(g)[:, :, at:at + n],
                                 wd[GROUPS[g][0]].rearrange("(k p) c -> p k c", p=P)[:, :, c:c + n]).then_inc(ws_in[g % 2], 16)
                    at += n

            sp.dma_start(X[:, 0, :], x[0:P, :]).then_inc(x_in[0], 16)
            sp.dma_start(ident, ident_d).then_inc(s["cst_in"], 16)
            sp.dma_start(prm_s, prm).then_inc(s["cst_in"], 16)
            for t in range(1, NT):
                sp.dma_start(X[:, t, :], x[t * P:(t + 1) * P, :]).then_inc(x_in[t], 16)
            sp.dma_start(XM[0:META, :], meta).then_inc(x_in[4], 16)
            load_group(0)
            sp.dma_start(tab, tab_d).then_inc(s["tab_in"], 16)
            load_group(1)
            sp.wait_ge(s["u_ready"], 5)
            sp.dma_start(UPW[:, 0:1536].rearrange("p (k c) -> p k c", k=2), w_uq.rearrange("(k p) c -> p k c", p=P)).then_inc(s["tab_in"], 16)
            sp.dma_start(UPW[:, 1536:2560], w_ukv).then_inc(s["tab_in"], 16)
            sp.dma_start(wr, w_router.rearrange("(k p) e -> p k e", p=P)).then_inc(s["tab_in"], 16)
            sp.dma_start(iota, iota_d).then_inc(s["tab_in"], 16)
            sp.dma_start(QT[QH:QH + NT], mask_d[:, 0:S].unsqueeze(1).to_broadcast([NT, MH, S])).then_inc(s["tab_in"], 16)
            sp.dma_start(KT[QH:QH + NT], mask_d[:, S:S + LT].unsqueeze(1).to_broadcast([NT, MH, LT])).then_inc(s["tab_in"], 16)
            for g in range(2, len(GROUPS)):
                load_group(g)
            sp.wait_ge(s["yt2_evac"], 4)
            sp.wait_ge(s["y2_done"], 4)
            w1v = w1.rearrange("e (k p) f -> e k p f", p=P)
            w3v = w3.rearrange("e (k p) f -> e k p f", p=P)
            w2v = w2.rearrange("e (h j p) d -> e j h p d", h=2, p=P)

            def expert_loads(e, w1_first):
                for k in range(KD):
                    if not w1_first:
                        sp.wait_ge(s["w13_used"], e * (2 * KD) - KD + k + 1)
                    sp.dma_start(W13[k], w1v[e, k]).then_inc(w13_in[k], 16)
                if w1_first:
                    for i in range(N2 - 4):
                        sp.dma_start(W2S[i], w2v[e, i // 2, i % 2]).then_inc(w2_in[i], 16)
                    sp.wait_ge(s["op2_psum"], 8)
                    for i in range(N2 - 4, N2):
                        sp.dma_start(W2S[i], w2v[e, i // 2, i % 2]).then_inc(w2_in[i], 16)
                for k in range(KD):
                    sp.wait_ge(s["w13_used"], e * (2 * KD) + k + 1)
                    sp.dma_start(W13[k], w3v[e, k]).then_inc(w13_in[k], 16)
                for i in range(N2 if w1_first else 0, 2 * N2):
                    sp.wait_ge(s["w2_used"], e * (2 * N2) - N2 + i + 1)
                    sp.dma_start(W2S[i % N2], w2v[e, i // 2, i % 2]).then_inc(w2_in[i % N2], 16)

            expert_loads(0, True)
            with sp.Fori(1, E) as e:
                expert_loads(e, False)
            for n in range(2 * NT):
                sp.wait_ge(s["sc_add"], (E - 1) * 2 * NT + n + 1)
                t, d = n // 2, n % 2
                sp.dma_start(out[t * P:(t + 1) * P, d * 512:(d + 1) * 512], X[:, t, d * 512:(d + 1) * 512]).then_inc(s["out_done"], 16)
            sp.wait_ge(s["out_done"], 16 * 2 * NT)

        @block.gpsimd
        def _(gp):
            own = Own(gp, s["gp_own"])
            gp.memset(ones, 1.0)
            gp.memset(eps, EPS)
            gp.memset(stat, 1.0)
            gp.memset(rstd, 1.0)
            gp.memset(var, 1.0)
            gp.memset(ms[0], 1.0)
            gp.memset(ms[1], 1.0)
            gp.memset(KR, 0.0).then_inc(s["gp_init"], 1)
            gp.wait_ge(s["tab_in"], 112)
            gp.wait_ge(s["cst_in"], 32)
            qs = QH ** -0.5

            def gain(name, n, t):
                return prm_c(name, 0, n).unsqueeze(1).to_broadcast([P, t, n])

            gp.tensor_tensor(rq_a, mcc[:, 0:4, :], gain("qr", 32, 4), ALU.mult)
            gp.tensor_tensor(rq_b, mss[:, 0:4, :], gain("qrs", 32, 4), ALU.mult)
            gp.tensor_tensor(rk_a, mcc, gain("kr", 32, 5), ALU.mult)
            gp.tensor_tensor(rk_b, mss, gain("krs", 32, 5), ALU.mult)
            gp.tensor_scalar(prm_c("qn"), prm_c("qn"), qs, None, ALU.mult).then_inc(s["gp_rope"], 1)
            gp.wait_ge(s["op_psum"], 1)
            own(gp.tensor_tensor(tq_a, bcc, gain("q2", 64, 4), ALU.mult))
            own(gp.tensor_tensor(tq_b, bss, gain("q2s", 64, 4), ALU.mult))
            gp.tensor_tensor(tk_a, bcc, gain("k2", 64, 4), ALU.mult)
            gp.tensor_tensor(tk_b, bss, gain("k2s", 64, 4), ALU.mult)
            own.settle()
            own(gp.tensor_scalar(tq_a, tq_a, HD ** -0.5, None, ALU.mult))
            own(gp.tensor_scalar(tq_b, tq_b, HD ** -0.5, None, ALU.mult))
            own.settle()
            gp.memset(LN_ONES, 1.0 / S)
            gp.memset(CU2[:, :, 0:PAD], 0.0)
            gp.memset(CU2[:, :, PAD + S:CW], 0.0).then_inc(s["pads"], 1)
            for m in range(2, 2 * TAPS):
                gp.wait_ge(s["tap_ready"], m + 1)
                if m >= 4:
                    gp.wait_ge(s["tap_added"], m - 3)
                acc = CA[:, m % 2, :]
                gp.tensor_tensor(acc, acc, TAP[m % 8], ALU.add).then_inc(s["tap_added"], 1)

        @block.scalar
        def _(act):
            own = Own(act, s["act_own"])

            def rsqrt_seed(y, sums, inv_n):
                own(act.activation(y, sums, ACT.Ln, bias=eps[0:y.shape[0], :], scale=inv_n))
                own.settle()
                return act.activation(y, y, ACT.Exp, scale=-0.5)

            act.preload_act_table_set("natural_log_exp_and_others")
            act.wait_ge(s["gp_init"], 1)
            for t in range(5):
                _, n = toks(t)
                src = X[:, t, :] if t < NT else XM[0:META, :]
                act.wait_ge(x_in[t], 16)
                if t >= 2:
                    act.wait_ge(s["ut_psum"], t - 1)
                own(act.activation(U[t % 2][0:n, :], src, ACT.Square, accum_out=stat[0:n, t:t + 1]))
                own.settle()
                rsqrt_seed(rstd[0:n, t:t + 1], stat[0:n, t:t + 1], 1.0 / D).then_inc(s["ustat"], 1)
            for b in range(4):
                act.wait_ge(s["lat_psum"], b + 1)
                src = PS[:, 4 + b, :] if b < 3 else PS[:, 7, 0:META]
                act.activation(SQ[:, b * 512:b * 512 + src.shape[1]], src, ACT.Square).then_inc(s["sq_ready"], 1)
            act.wait_ge(s["ut_ready"], 5)
            act.wait_ge(s["stat_psum"], 1)
            own(act.activation(rstd[:, 0:4], PS[:, 7, 32:36], ACT.Ln, bias=eps, scale=1.0 / 256))
            own(act.activation(rstd[:, 4:8], PS[:, 7, 36:40], ACT.Ln, bias=eps, scale=1.0 / 128))
            own(act.activation(rstd[0:META, 8:9], PS[0:META, 7, 40:41], ACT.Ln, bias=eps[0:META, :], scale=1.0 / 128))
            own.settle()
            act.activation(rstd, rstd, ACT.Exp, scale=-0.5).then_inc(s["lat_exp"], 1)
            for t in range(NT):
                act.wait_ge(s["mz_psum"], t + 1)
                if t >= 2:
                    act.wait_ge(s["mz_free"], t - 1)
                act.activation(SCR[:, (t % 2) * 512:(t % 2) * 512 + 512], PS[:, t % 2, :], ACT.Exp, scale=-1.0).then_inc(s["mz_exp"], 1)
            act.wait_ge(s["lat_rstd"], 1)

            def evac(t):
                _, n = toks(t)
                act.wait_ge(s["qk_psum"], t + 1)
                if t >= 2:
                    act.wait_ge(s["kT_psum"], t - 1)
                if t >= 1:
                    act.wait_ge(s["ms_ready"], t)
                if t < NT:
                    q = PS[:, 3:5, 0:384]
                    act.activation(QTOK[t % 2].rearrange("p (b c) -> p b c", b=2), q, ACT.Copy, scale=rstd[:, t:t + 1])
                    act.activation(QSQ[:, 0:768].rearrange("p (b c) -> p b c", b=2), q, ACT.Square, scale=rstd[:, t:t + 1])
                kv = PF[0:n, 5 * 512:7 * 512].rearrange("p (h c) -> p h c", h=MH)
                r = rstd[0:n, 4 + t:5 + t]
                act.activation(KTOK[t % 2][0:n, :].rearrange("p (h c) -> p h c", h=MH)[:, :, 0:NOPE], kv[:, :, 0:NOPE], ACT.Copy, scale=r)
                act.activation(QSQ[0:n, 768:1280].rearrange("p (h c) -> p h c", h=MH), kv[:, :, 0:NOPE], ACT.Square, scale=r)
                act.activation(V1[0:n, t * 512:(t + 1) * 512].rearrange("p (h c) -> p h c", h=MH), kv[:, :, NOPE:128], ACT.Copy,
                               scale=r).then_inc(s["qk_evac"], 1)

            def head_stats(t):
                _, n = toks(t)
                act.wait_ge(s["ms_ready"], t + 1)
                if t >= 2:
                    act.wait_ge(s["k_ready"], t - 1)
                a = 0 if t < NT else 8
                rsqrt_seed(rs[t % 2][0:n, a:16], ms[t % 2][0:n, a:16], 1.0 / QH).then_inc(s["ms_exp"], 1)

            def qT_out(t):
                act.wait_ge(s["qT_psum"], t + 1)
                for f in range(2):
                    i = act.activation(QT[0:QH, 4 * f:4 * f + 4, t * P:(t + 1) * P],
                                       PS[0:QH, f, :].rearrange("p (h c) -> p h c", h=4), ACT.Copy, scale=prm_c("qn")[0:QH, :])
                i.then_inc(s["qT_evac"], 1)

            def rrT_out(t):
                c, n = toks(t)
                act.wait_ge(s["rrT_psum"], t + 1)
                ps = PS[:, 0, :].rearrange("p (j c) -> p j c", j=4)
                if t < NT:
                    act.activation(RQT[:, :, c:c + n], ps[:, 0:2, :], ACT.Copy)
                act.activation(RKT[:, :, c:c + n], ps[:, 2:4, 0:n], ACT.Copy).then_inc(s["rrT_evac"], 1)

            evac(0), head_stats(0), evac(1), head_stats(1), qT_out(0), evac(2), head_stats(2)
            rrT_out(0), qT_out(1), evac(3), head_stats(3), rrT_out(1), qT_out(2), evac(4), head_stats(4)
            rrT_out(2), qT_out(3), rrT_out(3), rrT_out(4)
            for t in range(5):
                _, n = toks(t)
                act.wait_ge(s["e_psum"], 6 + t)
                act.activation(RV[0:n, t * 256:(t + 1) * 256], PS[0:n, [2, 7][(5 + t) % 2], 0:256], ACT.Copy).then_inc(s["rv_evac"], 1)
            for j in range(2):
                act.wait_ge(s["e_psum"], 11 + j)
                act.activation(SCR[:, j * 512:(j + 1) * 512], PS[:, [2, 7][j], :], ACT.Exp, scale=-1.0).then_inc(s["rz_exp"], 1)
            for j in range(2):
                act.wait_ge(s["ro_psum"], j + 1)
                act.activation(RSQ[j], PS[:, 6 + j, :], ACT.Square).then_inc(s["ro_sq"], 1)
            for j in range(2):
                act.wait_ge(s["ro_v"], j + 1)
                own(act.activation(RFAC[j], RVAR[j], ACT.Ln))
                own.settle()
                act.activation(RFAC[j], RFAC[j], ACT.Exp, scale=-0.5).then_inc(s["ro_exp"], 1)
            act.wait_ge(s["ro_psum"], 2)
            for b in range(2):
                act.wait_ge(s["f_psum"], 2 * b + 1)
                act.activation(CU1[:, b, 0:2], PS[:, 2 * b, 0:2], ACT.Copy)
                act.activation(CU1[:, b, 2:S + 2], PS[:, 3 + 2 * b, :], ACT.Copy).then_inc(s["cc_evac"], 1)
            for b in range(2):
                act.wait_ge(s["f_psum"], 4 + 2 * b + 1)
                act.activation(SCR[:, b * 512:b * 512 + 512], PS[:, 3 + 2 * b, :], ACT.Exp, scale=-1.0).then_inc(s["cz_exp"], 1)
            def probs(i):
                t = i // MH
                b = score_bank(i)
                n = (t + 1) * P + META
                act.wait_ge(s["nm_ready"], i + 1)
                if i >= 6:
                    act.wait_ge(s["pt_psum"], i // 2 - 2)
                act.activation(PB[i % 6][:, 0:n], PF[:, b * 512:b * 512 + n], ACT.Exp, bias=nmax[:, i % 4:i % 4 + 1],
                               accum_out=lsum[:, i:i + 1]).then_inc(s["p_done"], 1)

            def pt_out(n):
                c = (n // 4 + 1) * P
                act.wait_ge(s["pt_psum"], n + 1)
                if n >= 1:
                    act.wait_ge(s["pv_psum"], n)
                act.activation(PT[:, :, 0:c], PS[:, 4:6, 0:c], ACT.Copy).then_inc(s["pt_evac"], 1)

            act.wait_ge(s["yr_ready"], 2)
            for n in range(NT * 4):
                probs(2 * n), probs(2 * n + 1)
                if n >= 1:
                    pt_out(n - 1)
            pt_out(NT * 4 - 1)

            for t in range(NT):
                act.wait_ge(s["xo_done"], 2 * t + 2)
                if t >= 2:
                    act.wait_ge(s["ut2_psum"], t - 1)
                own(act.activation(U2[t % 2], X[:, t, :], ACT.Square, accum_out=stat[:, t:t + 1]))
                own.settle()
                rsqrt_seed(rstd[:, t:t + 1], stat[:, t:t + 1], 1.0 / D).then_inc(s["ustat2"], 1)
            for j in range(4):
                act.wait_ge(s["f2_psum"], 2 * j + 1)
                if j >= 2:
                    act.wait_ge(s["cu_done"], j - 1)
                act.activation(SCB[j % 2], PS[:, (2 * j) % 4, :], ACT.Exp, scale=-1.0).then_inc(s["b_exp"], 1)

            def zT_out(i):
                t = i % NT
                act.wait_ge(s["zT_psum"], i + 1)
                dst = QT2 if i < NT else KT2
                act.activation(dst[:, :, t * P:(t + 1) * P], PS[:, i % 2, :].rearrange("p (j c) -> p j c", j=4), ACT.Copy)\
                    .then_inc(s["zT_evac"], 1)

            taps_done = 0

            def tap_products(n):
                for m in range(taps_done, min(taps_done + n, 2 * TAPS)):
                    j, b = m // 2, m % 2
                    w = prm_c("dw", b * TAPS + j)
                    if j == 0:
                        act.wait_ge(s["cu_done"], 4)
                        act.activation(CA[:, b, :], CU2[:, b, 0:S], ACT.Identity, scale=w, bias=prm_c("dwb", b)).then_inc(s["tap_ready"], 1)
                    else:
                        if m >= 10:
                            act.wait_ge(s["tap_added"], m - 9)
                        act.activation(TAP[m % 8], CU2[:, b, j:j + S], ACT.Copy, scale=w).then_inc(s["tap_ready"], 1)
                return min(taps_done + n, 2 * TAPS)

            for i in range(2 * NT):
                act.wait_ge(s["z_psum"], i + 1)
                if i >= 1:
                    act.wait_ge(s["z_ms"], i)
                act.activation(XSQ, PS[:, 4 + i % 4, :], ACT.Square).then_inc(s["z_sq"], 1)
                act.wait_ge(s["z_ms"], i + 1)
                rsqrt_seed(rs[i % 2][:, 0:8], ms[i % 2][:, 0:8], 1.0 / HD).then_inc(s["z_rs"], 1)
                if i >= 1:
                    zT_out(i - 1)
                taps_done = tap_products(PRODUCTS_PER_TILE)
            zT_out(2 * NT - 1)
            taps_done = tap_products(2 * TAPS)
            for t in range(NT):
                act.wait_ge(s["z_psum"], 2 * NT + 1 + t)
                act.activation(V2[:, t * 512:(t + 1) * 512], PS[:, 4 + t % 4, :], ACT.Copy).then_inc(s["v_evac"], 1)

            def probs2(i):
                act.wait_ge(s["nm2_ready"], i + 1)
                act.activation(SM[i % 6], SM[i % 6], ACT.Exp, scale=-1.0, bias=nmax[:, i % 4:i % 4 + 1],
                               accum_out=lsum[:, i:i + 1]).then_inc(s["p2_done"], 1)

            def pt2_out(n):
                act.wait_ge(s["pt2_psum"], n + 1)
                if n >= 1:
                    act.wait_ge(s["pv2_psum"], n)
                act.activation(PT2, PS[:, 4:6, :], ACT.Copy).then_inc(s["pt2_evA"], 1)

            def yt2_out(t):
                act.wait_ge(s["pv2_psum"], 4 * (t + 1))
                act.activation(YT2[:, 0:4, t * P:(t + 1) * P], PS[:, 6, :].rearrange("p (j c) -> p j c", j=4), ACT.Copy)\
                    .then_inc(s["yt2_evac"], 1)

            for n in range(NT * 4):
                probs2(2 * n), probs2(2 * n + 1)
                if n >= 1:
                    pt2_out(n - 1)
                if n == 5:
                    act.wait_ge(s["tap_added"], 2 * TAPS - 2)
                if n % 4 == 1 and n > 4:
                    yt2_out(n // 4 - 1)
                if n == LN_AT + 1:
                    for j in range(4):
                        act.wait_ge(s["cen_done"], j + 1)
                        act.activation(LSQ[:, j, :], CA[:, j, :], ACT.Square).then_inc(s["lsq_done"], 1)
                if n == LN_AT + 2:
                    act.wait_ge(s["lv_ready"], 1)
                    own(act.activation(LY, LV, ACT.Ln))
                    own.settle()
                    act.activation(LY, LY, ACT.Exp, scale=-0.5).then_inc(s["lrs_done"], 1)
                if n >= LN_AT + 3 and n < LN_AT + 7:
                    j = n - LN_AT - 3
                    act.wait_ge(s["ly_ready"], j + 1)
                    if j >= 2:
                        act.wait_ge(s["y2_done"], j - 1)
                    act.activation(SCB[j % 2], CA[:, j, :], ACT.Exp, scale=-1.0).then_inc(s["ly_exp"], 1)
            pt2_out(NT * 4 - 1)
            yt2_out(NT - 1)

            for t in range(NT):
                act.wait_ge(s["xo2_done"], 2 * t + 2)
                if t >= 2:
                    act.wait_ge(s["h2T_psum"], t - 1)
                own(act.activation(HR[t % 2], X[:, t, :], ACT.Square, accum_out=stat[:, t:t + 1]))
                own.settle()
                rsqrt_seed(rstd[:, t:t + 1], stat[:, t:t + 1], 1.0 / D).then_inc(s["rstat"], 1)
            act.wait_ge(s["h2_ready"], NT)
            act.wait_ge(s["op2_psum"], 8)
            for t in range(NT - 1):
                act.activation(H2N[:, t, :], X[:, t, :], ACT.Copy, scale=rstd[:, t:t + 1]).then_inc(s["h2n_ready"], 1)
            act.wait_ge(s["lg_sub"], 1)
            act.activation(AEX, AEX, ACT.Exp).then_inc(s["lg_exp"], 1)
            act.activation(H2N[:, NT - 1, :], X[:, NT - 1, :], ACT.Copy, scale=rstd[:, NT - 1:NT]).then_inc(s["h2n_ready"], 1)
            act.preload_act_table(ACT.Silu)

            def expert(e, first):
                act.wait_ge(s["w13_used"], e * (2 * KD) + KD)
                if not first:
                    act.wait_ge(s["hh_done"], e)
                act.activation(S1, PF[:, 0:FH], ACT.Silu).then_inc(s["s1_done"], 1)
                act.wait_ge(s["ht_psum"], e + 1)
                act.activation(HT[:, 0:4, :], PF[:, 0:4 * P].rearrange("p (j c) -> p j c", j=4), ACT.Copy).then_inc(s["ht_evA"], 1)

            expert(0, True)
            with act.Fori(1, E) as e:
                expert(e, False)

        @block.vector
        def _(dve):
            own = Own(dve, s["dve_own"])

            def refine(y, sums, inv_n, have_v=None, signal=None):
                n, w = y.shape
                v, a = var[0:n, 0:w], newt[0:n, 0:w]
                if have_v is None:
                    own(dve.tensor_scalar(v, sums, inv_n, EPS, ALU.mult, ALU.add))
                own(dve.tensor_tensor(a, y, y, ALU.mult))
                own.settle()
                own(dve.scalar_tensor_tensor(a, a, -0.5, v, ALU.mult, ALU.mult))
                own.settle()
                i = dve.scalar_tensor_tensor(y, a, 1.5, y, ALU.add, ALU.mult)
                if signal:
                    i.then_inc(s[signal], 1)
                else:
                    own(i)
                    own.settle()

            def bc(ap, n):
                return ap.unsqueeze(2).to_broadcast([ap.shape[0], ap.shape[1], n])

            def rows(ap, h):
                return ap.unsqueeze(1).to_broadcast([ap.shape[0], h, ap.shape[1]])

            dve.wait_ge(s["gp_init"], 1)
            dve.wait_ge(s["cst_in"], 32)
            for t in range(6):
                if t < 5:
                    _, n = toks(t)
                    dve.wait_ge(s["ustat"], t + 1)
                    refine(rstd[0:n, t:t + 1], stat[0:n, t:t + 1], 1.0 / D)
                    src = X[:, t, :] if t < NT else XM[0:META, :]
                    dve.tensor_scalar(U[t % 2][0:n, :], src, rstd[0:n, t:t + 1], None, ALU.mult).then_inc(s["u_ready"], 1)
                if t >= 1:
                    c, n = toks(t - 1)
                    dve.wait_ge(s["ut_psum"], t)
                    for f in range(2):
                        i = dve.tensor_tensor(UT[:, 4 * f:4 * f + 4, c:c + n],
                                              PS[:, 2 * ((t - 1) % 2) + f, :].rearrange("p (k c) -> p k c", k=4)[:, :, 0:n],
                                              bc(prm_c("lnw", 4 * f, 4), n), ALU.mult)
                    i.then_inc(s["ut_ready"], 1)
            for b in range(4):
                dve.wait_ge(s["sq_ready"], b + 1)
                if b < 2:
                    i = dve.tensor_scalar(CQT[:, b * S:(b + 1) * S], PS[:, 4 + b, :], prm_c("qan", b), None, ALU.mult)
                elif b == 2:
                    i = dve.tensor_scalar(CKVT[:, 0:S], PS[:, 6, :], prm_c("kvan"), None, ALU.mult)
                else:
                    i = dve.tensor_scalar(CKVT[:, S:LT], PS[:, 7, 0:META], prm_c("kvan"), None, ALU.mult)
                i.then_inc(s["lat_ready"], 1)
            dve.wait_ge(s["kr_psum"], 1)
            dve.wait_ge(s["gp_rope"], 1)
            own(dve.tensor_copy(KR[:, 0:4, :], PS[:, 2, 0:128].rearrange("p (t c) -> p t c", t=4)))
            dve.tensor_copy(KR[0:META, 4, :], PS[0:META, 2, 128:160]).then_inc(s["kr_copied"], 1)
            dve.wait_ge(s["kr_copied"], 1)
            own(dve.tensor_tensor(KRQ, KR, KR, ALU.mult))
            own.settle()
            own(dve.tensor_reduce(krs, KRQ, AX.X, ALU.add))
            own.settle()
            own(dve.tensor_tensor(KRQ[:, :, 0:16], KR[:, :, 16:32], rk_b[:, :, 0:16], ALU.mult))
            own(dve.tensor_tensor(KRQ[:, :, 16:32], KR[:, :, 0:16], rk_b[:, :, 16:32], ALU.mult))
            own(dve.tensor_tensor(KRT, KR, rk_a, ALU.mult))
            own.settle()
            own(dve.tensor_tensor(KRG, KRQ, KRT, ALU.add))
            dve.wait_ge(s["lat_exp"], 1)
            own(dve.tensor_scalar(var[:, 0:4], PS[:, 7, 32:36], 1.0 / 256, EPS, ALU.mult, ALU.add))
            own(dve.tensor_scalar(var[:, 4:8], PS[:, 7, 36:40], 1.0 / 128, EPS, ALU.mult, ALU.add))
            own(dve.tensor_scalar(var[0:META, 8:9], PS[0:META, 7, 40:41], 1.0 / 128, EPS, ALU.mult, ALU.add))
            refine(rstd, None, None, have_v=True, signal="lat_rstd")

            def silu(e, z, dst):
                own(dve.tensor_scalar(e, e, 1.0, None, ALU.add))
                own.settle()
                own(dve.reciprocal(e, e))
                own.settle()
                return dve.tensor_tensor(dst, e, z, ALU.mult)

            for t in range(NT):
                dve.wait_ge(s["mz_exp"], t + 1)
                silu(SCR[:, (t % 2) * 512:(t % 2) * 512 + 512], PS[:, t % 2, :], MZ[:, t * 512:(t + 1) * 512]).then_inc(s["mz_free"], 1)

            def reduce_heads(t):
                _, n = toks(t)
                dve.wait_ge(s["qk_evac"], t + 1)
                if t >= 2:
                    dve.wait_ge(s["ms_exp"], t - 1)
                m = ms[t % 2]
                own(dve.tensor_reduce(m[0:n, 8:16], QSQ[0:n, 768:1280].rearrange("p (h c) -> p h c", h=MH), AX.X, ALU.add))
                if t < NT:
                    own(dve.tensor_reduce(m[:, 0:8], QSQ[:, 0:768].rearrange("p (h c) -> p h c", h=MH), AX.X, ALU.add))
                own.settle()
                dve.tensor_scalar(m[0:n, 8:16], m[0:n, 8:16], krs[0:n, t:t + 1], None, ALU.add).then_inc(s["ms_ready"], 1)

            def apply_heads(t):
                _, n = toks(t)
                dve.wait_ge(s["ms_exp"], t + 1)
                dve.wait_ge(s["ms_ready"], t + 1)
                r = rs[t % 2]
                a = 0 if t < NT else 8
                refine(r[0:n, a:16], ms[t % 2][0:n, a:16], 1.0 / QH)
                if t < NT:
                    q = QTOK[t % 2].rearrange("p (h c) -> p h c", h=MH)
                    own(dve.tensor_tensor(q, q, bc(r[:, 0:8], QH), ALU.mult))
                    own.settle()
                    if t >= 1:
                        dve.wait_ge(s["rrT_psum"], t)
                    t1 = RT1[:, 0:256].rearrange("p (h c) -> p h c", h=MH)
                    t2 = RT2[:, 0:256].rearrange("p (h c) -> p h c", h=MH)
                    own(dve.tensor_tensor(t1, q[:, :, 64:96], rows(rq_a[:, t, :], MH), ALU.mult))
                    own(dve.tensor_tensor(t2[:, :, 0:16], q[:, :, 80:96], rows(rq_b[:, t, 0:16], MH), ALU.mult))
                    own(dve.tensor_tensor(t2[:, :, 16:32], q[:, :, 64:80], rows(rq_b[:, t, 16:32], MH), ALU.mult))
                    own.settle()
                    dve.tensor_tensor(q[:, :, 64:96], t1, t2, ALU.add).then_inc(s["q_ready"], 1)
                k = KTOK[t % 2][0:n, :].rearrange("p (h c) -> p h c", h=MH)
                own(dve.tensor_tensor(k[:, :, 0:NOPE], k[:, :, 0:NOPE], bc(r[0:n, 8:16], NOPE), ALU.mult))
                dve.tensor_tensor(k[:, :, 64:96], rows(KRG[0:n, t, :], MH), bc(r[0:n, 8:16], ROPE), ALU.mult).then_inc(s["k_ready"], 1)

            def kT_out(t):
                _, n = toks(t)
                kc = META + t * P if t < NT else 0
                dve.wait_ge(s["kT_psum"], t + 1)
                for f in range(2):
                    i = dve.tensor_scalar(KT[0:QH, 4 * f:4 * f + 4, kc:kc + n],
                                          PS[0:QH, f, :].rearrange("p (h c) -> p h c", h=4)[:, :, 0:n], prm_c("kn")[0:QH, :], None, ALU.mult)
                i.then_inc(s["kT_evac"], 1)

            def rotate(t):
                _, n = toks(t)
                dve.wait_ge(s["e_psum"], t + 1)
                if t >= 1:
                    dve.wait_ge(s["rrT_psum"], t)
                if t < NT:
                    dve.wait_ge(s["q_ready"], t + 1)
                b = [2, 7][t % 2]
                h = 8 if t < NT else 4
                o = 0 if t < NT else 256
                src = PS[0:n, b, o:512].rearrange("p (h c) -> p h c", h=h)
                t1 = RT1[0:n, o:512].rearrange("p (h c) -> p h c", h=h)
                t2 = RT2[0:n, o:512].rearrange("p (h c) -> p h c", h=h)
                own(dve.tensor_tensor(t1, src, rows(rcc[0:n, t, :], h), ALU.mult))
                own(dve.tensor_tensor(t2[:, :, 0:32], src[:, :, 32:64], rows(rss[0:n, t, 0:32], h), ALU.mult))
                dve.tensor_tensor(t2[:, :, 32:64], src[:, :, 0:32], rows(rss[0:n, t, 32:64], h), ALU.mult).then_inc(s["e_free"], 1)
                dve.wait_ge(s["e_free"], t + 1)
                own.settle()
                dve.tensor_tensor(t1, t1, t2, ALU.add).then_inc(s["rr_ready"], 1)

            reduce_heads(0), reduce_heads(1), apply_heads(0), rotate(0), kT_out(0), reduce_heads(2)
            apply_heads(1), rotate(1), kT_out(1), reduce_heads(3), apply_heads(2), rotate(2), kT_out(2), reduce_heads(4)
            apply_heads(3), rotate(3), kT_out(3), apply_heads(4), rotate(4), kT_out(4)
            for j in range(2):
                dve.wait_ge(s["rz_exp"], j + 1)
                silu(SCR[:, j * 512:(j + 1) * 512], PS[:, [2, 7][j], :], SRZ[:, j * 512:(j + 1) * 512]).then_inc(s["e_free"], 1)
            dve.wait_ge(s["kT_psum"], 5)
            dve.wait_ge(s["rrT_psum"], 5)
            dve.wait_ge(s["e_free"], 7)
            for h in range(RH):
                for b in range(5):
                    i = 5 * h + b
                    dve.wait_ge(s["rs_psum"], i + 1)
                    if b < NT:
                        n = S - b * P
                        o = [0, 512, 896, 1152][b]
                        ins = dve.tensor_tensor(SD[h][:, o:o + n], PS[:, i % 4, 0:n], dec[:, h, 0:n], ALU.mult)
                    else:
                        ins = dve.tensor_tensor(SD[h][0:META, 1280:1792], PS[0:META, i % 4, :], dec[0:META, h, META:LT], ALU.mult)
                    ins.then_inc(s["ret_s"], 1)
            for j in range(2):
                dve.wait_ge(s["ro_ms"], j + 1)
                dve.tensor_scalar(RVAR[j], PS[:, 4 + j, :], EPS, None, ALU.add).then_inc(s["ro_v"], 1)
                dve.wait_ge(s["ro_exp"], j + 1)
                dve.wait_ge(s["ro_v"], j + 1)
                own(dve.tensor_tensor(RTMP, RFAC[j], RFAC[j], ALU.mult))
                own.settle()
                own(dve.scalar_tensor_tensor(RTMP, RTMP, -0.5, RVAR[j], ALU.mult, ALU.mult))
                own.settle()
                own(dve.scalar_tensor_tensor(RFAC[j], RTMP, 1.5, RFAC[j], ALU.add, ALU.mult))
                own.settle()
                own(dve.scalar_tensor_tensor(RFAC[j], PS[:, 6 + j, :], prm_c("retc"), RFAC[j], ALU.mult, ALU.mult))
                own.settle()
                z = SRZ[:, j * 512:(j + 1) * 512]
                dve.tensor_tensor(z, RFAC[j], z, ALU.mult).then_inc(s["yr_ready"], 1)
            for b in range(2):
                dve.wait_ge(s["cc_evac"], b + 1)
                dve.wait_ge(s["f_psum"], 2 * b + 2)
                own(dve.tensor_tensor(CU1[:, b, 0:2], CU1[:, b, 0:2], PS[:, [1, 7][b], 0:2], ALU.mult))
                dve.tensor_tensor(CU1[:, b, 2:S + 2], CU1[:, b, 2:S + 2], PS[:, 4 + 2 * b, :], ALU.mult).then_inc(s["cx_done"], 1)
            for b in range(2):
                dve.wait_ge(s["cz_exp"], b + 1)
                own(silu(SCR[:, b * 512:b * 512 + 512], PS[:, 3 + 2 * b, :], CG[:, b, :]))
                own.settle()
                dve.wait_ge(s["f_psum"], 4 + 2 * b + 2)
                dve.tensor_tensor(CG[:, b, :], CG[:, b, :], PS[:, 4 + 2 * b, :], ALU.mult).then_inc(s["cz_done"], 1)

            def conv_ops():
                dve.wait_ge(s["cx_done"], 2)
                dve.wait_ge(s["cz_done"], 2)
                dve.wait_ge(s["ro_psum"], 2)
                acc = [RT1, RT2]
                for j in range(3):
                    for b in range(2):
                        w = prm_c("cw", b * 3 + j)
                        if j == 0:
                            own(dve.tensor_scalar(acc[b], CU1[:, b, 0:S], w, prm_c("cb", b), ALU.mult, ALU.add))
                        else:
                            own.settle(conv_last[b])
                            own(dve.scalar_tensor_tensor(acc[b], CU1[:, b, j:j + S], w, acc[b], ALU.mult, ALU.add))
                        conv_last[b] = own.n
                        yield
                for b in range(2):
                    own.settle(conv_last[b])
                    dve.tensor_tensor(YT[:, b, :], acc[b], CG[:, b, :], ALU.mult).then_inc(s["conv_y"], 1)
                    yield

            conv_last = [0, 0]
            conv = conv_ops()

            def row_max(i):
                t, b = i // MH, score_bank(i)
                n = (t + 1) * P + META
                dve.wait_ge(s["s_psum"], i + 1)
                if i >= 4:
                    dve.wait_ge(s["p_done"], i - 3)
                dve.tensor_reduce(nmax[:, i % 4:i % 4 + 1], PF[:, b * 512:b * 512 + n], AX.X, ALU.max, negate=True).then_inc(s["nm_ready"], 1)

            def norm_p(n):
                c = (n // 4 + 1) * P + META
                li = linv[:, 2 * n:2 * n + 2]
                dve.wait_ge(s["p_done"], 2 * n + 2)
                own(dve.reciprocal(li, lsum[:, 2 * n:2 * n + 2]))
                own.settle()
                for f in range(2):
                    p = PB[(2 * n + f) % 6][:, 0:c]
                    i = dve.tensor_scalar(p, p, li[:, f:f + 1], None, ALU.mult)
                i.then_inc(s["ps_ready"], 1)

            def ptm_out(n):
                dve.wait_ge(s["pt_psum"], n + 1)
                if n >= 1:
                    dve.wait_ge(s["pv_psum"], n)
                dve.tensor_copy(PTM[0:META], PS[0:META, 6, 0:256].rearrange("p (f c) -> p f c", f=2)).then_inc(s["ptm_evac"], 1)

            def tile_out(t):
                dve.wait_ge(s["pv_psum"], 4 * (t + 1))
                dve.tensor_tensor(YT[:, 2:6, t * P:(t + 1) * P], PS[:, 7, :].rearrange("p (j c) -> p j c", j=4),
                                  MZ.rearrange("p (j c) -> p j c", j=4)[:, :, t * P:(t + 1) * P], ALU.mult).then_inc(s["yo_free"], 1)

            row_max(0), row_max(1)
            for n in range(NT * 4):
                if n >= 1:
                    ptm_out(n - 1)
                norm_p(n)
                if n + 1 < NT * 4:
                    row_max(2 * n + 2), row_max(2 * n + 3)
                if n % 4 == 0 and n > 0:
                    tile_out(n // 4 - 1)
                next(conv, None)
            ptm_out(NT * 4 - 1)
            tile_out(NT - 1)
            def residual(i):
                t, n = i // 2, i % 2
                dve.wait_ge(s["op_psum"], i + 1)
                xs = X[:, t, n * 512:(n + 1) * 512]
                dve.tensor_tensor(xs, xs, PS[:, i % 4, :], ALU.add).then_inc(s["xo_done"], 1)

            def norm_row(t):
                dve.wait_ge(s["ustat2"], t + 1)
                refine(rstd[:, t:t + 1], stat[:, t:t + 1], 1.0 / D)
                dve.tensor_scalar(U2[t % 2], X[:, t, :], rstd[:, t:t + 1], None, ALU.mult).then_inc(s["u2_ready"], 1)

            def rowT_out(t):
                c = t * P
                dve.wait_ge(s["ut2_psum"], t + 1)
                for f in range(2):
                    i = dve.tensor_tensor(UT2[:, 4 * f:4 * f + 4, c:c + P],
                                          PS[:, 4 + 2 * (t % 2) + f, :].rearrange("p (k c) -> p k c", k=4),
                                          bc(prm_c("n1g", 4 * f, 4), P), ALU.mult)
                i.then_inc(s["ut2_ready"], 1)

            for t in range(NT):
                residual(2 * t)
                if t >= 1:
                    rowT_out(t - 1)
                residual(2 * t + 1)
                norm_row(t)
            rowT_out(NT - 1)
            dve.wait_ge(s["pads"], 1)
            for j in range(4):
                dve.wait_ge(s["b_exp"], j + 1)
                dve.wait_ge(s["f2_psum"], 2 * j + 2)
                silu(SCB[j % 2], PS[:, (2 * j + 1) % 4, :], CU2[:, j, PAD:PAD + S]).then_inc(s["cu_done"], 1)

            def taps_ops():
                dve.wait_ge(s["cu_done"], 4)
                for j in range(TAPS):
                    for b in (2, 3):
                        w = prm_c("dw", b * TAPS + j)
                        if j == 0:
                            own(dve.tensor_scalar(CA[:, b, :], CU2[:, b, 0:S], w, prm_c("dwb", b), ALU.mult, ALU.add))
                        else:
                            own.settle(last[b])
                            i = dve.scalar_tensor_tensor(CA[:, b, :], CU2[:, b, j:j + S], w, CA[:, b, :], ALU.mult, ALU.add)
                            if j < TAPS - 1:
                                own(i)
                            else:
                                i.then_inc(s["cv_done"], 1)
                        last[b] = own.n
                        yield

            last = {}
            ops = taps_ops()

            def some_taps(n):
                for _ in range(n):
                    next(ops, None)

            for i in range(2 * NT):
                t = i % NT
                ta, tb = (tq_a, tq_b) if i < NT else (tk_a, tk_b)
                dve.wait_ge(s["z_sq"], i + 1)
                if i >= 2:
                    dve.wait_ge(s["z_rs"], i - 1)
                dve.tensor_reduce(ms[i % 2][:, 0:8], XSQ.rearrange("p (h c) -> p h c", h=H2), AX.X, ALU.add).then_inc(s["z_ms"], 1)
                some_taps(TAPS_PER_TILE)
                dve.wait_ge(s["z_rs"], i + 1)
                dve.wait_ge(s["z_ms"], i + 1)
                refine(rs[i % 2][:, 0:8], ms[i % 2][:, 0:8], 1.0 / HD)
                xn = XN.rearrange("p (h c) -> p h c", h=H2)
                t1 = XT1.rearrange("p (h c) -> p h c", h=H2)
                t2 = XT2.rearrange("p (h c) -> p h c", h=H2)
                dve.tensor_tensor(xn, PS[:, 4 + i % 4, :].rearrange("p (h c) -> p h c", h=H2), bc(rs[i % 2][:, 0:8], HD), ALU.mult)\
                    .then_inc(s["z_free"], 1)
                dve.wait_ge(s["z_free"], i + 1)
                if i >= 1:
                    dve.wait_ge(s["zT_psum"], i)
                own(dve.tensor_tensor(t1, xn, rows(ta[:, t, :], H2), ALU.mult))
                own(dve.tensor_tensor(t2[:, :, 0:32], xn[:, :, 32:64], rows(tb[:, t, 0:32], H2), ALU.mult))
                own(dve.tensor_tensor(t2[:, :, 32:64], xn[:, :, 0:32], rows(tb[:, t, 32:64], H2), ALU.mult))
                own.settle()
                dve.tensor_tensor(t1, t1, t2, ALU.add).then_inc(s["zr_ready"], 1)
            for _ in ops:
                pass

            def row_max2(i):
                t = i // H2
                dve.wait_ge(s["s2_psum"], i + 1)
                if i >= 6:
                    dve.wait_ge(s["pt2_psum"], i // 2 - 2)
                if i >= 4:
                    dve.wait_ge(s["p2_done"], i - 3)
                dve.tensor_tensor_reduce(out=SM[i % 6], in0=PS[:, 2 * (i // 2 % 2) + i % 2, :], in1=cm[:, S - P - t * P:2 * S - P - t * P], scale=-1.0,
                                         scalar=3.0e38, op0=ALU.add, op1=ALU.min, accum_out=nmax[:, i % 4:i % 4 + 1]).then_inc(s["nm2_ready"], 1)

            def norm_p2(n):
                li = linv[:, 2 * n:2 * n + 2]
                dve.wait_ge(s["p2_done"], 2 * n + 2)
                own(dve.reciprocal(li, lsum[:, 2 * n:2 * n + 2]))
                own.settle()
                for f in range(2):
                    p = SM[(2 * n + f) % 6]
                    ins = dve.tensor_scalar(p, p, li[:, f:f + 1], None, ALU.mult)
                ins.then_inc(s["ps2_ready"], 1)

            row_max2(0), row_max2(1)
            for n in range(NT * 4):
                norm_p2(n)
                if n + 1 < NT * 4:
                    row_max2(2 * n + 2), row_max2(2 * n + 3)
                if n == LN_AT + 1:
                    dve.wait_ge(s["mean_psum"], 1)
                    dve.wait_ge(s["cv_done"], 2)
                    dve.wait_ge(s["tap_added"], 2 * TAPS - 2)
                    for j in range(4):
                        dve.tensor_tensor(CA[:, j, :], CA[:, j, :], PS[:, 7, :], ALU.subtract).then_inc(s["cen_done"], 1)
                if n == LN_AT + 2:
                    dve.wait_ge(s["var_psum"], 1)
                    dve.tensor_scalar(LV, PS[:, 7, :], EPS, None, ALU.add).then_inc(s["lv_ready"], 1)
                if n == LN_AT + 3:
                    dve.wait_ge(s["lrs_done"], 1)
                    own(dve.tensor_tensor(LA, LY, LY, ALU.mult))
                    own.settle()
                    own(dve.scalar_tensor_tensor(LA, LA, -0.5, LV, ALU.mult, ALU.mult))
                    own.settle()
                    own(dve.scalar_tensor_tensor(LY, LA, 1.5, LY, ALU.add, ALU.mult))
                if LN_AT + 3 <= n < LN_AT + 7:
                    j = n - LN_AT - 3
                    own.settle()
                    dve.wait_ge(s["cen_done"], 4)
                    dve.wait_ge(s["lsq_done"], 4)
                    own(dve.tensor_tensor(CA[:, j, :], CA[:, j, :], LY, ALU.mult))
                    own.settle()
                    dve.tensor_scalar(CA[:, j, :], CA[:, j, :], prm_c("lng", j), prm_c("lnb", j), ALU.mult, ALU.add).then_inc(s["ly_ready"], 1)
                if LN_AT + 4 <= n < LN_AT + 8:
                    j = n - LN_AT - 4
                    dve.wait_ge(s["ly_exp"], j + 1)
                    silu(SCB[j % 2], CA[:, j, :], YT2[:, 4 + j, :]).then_inc(s["y2_done"], 1)
            def residual2(i):
                t, n = i // 2, i % 2
                dve.wait_ge(s["op2_psum"], i + 1)
                xs = X[:, t, n * 512:(n + 1) * 512]
                dve.tensor_tensor(xs, xs, PS[:, i % 4, :], ALU.add).then_inc(s["xo2_done"], 1)

            def router_row(t):
                dve.wait_ge(s["rstat"], t + 1)
                refine(rstd[:, t:t + 1], stat[:, t:t + 1], 1.0 / D)
                dve.tensor_scalar(HR[t % 2], X[:, t, :], rstd[:, t:t + 1], None, ALU.mult).then_inc(s["h2_ready"], 1)

            def router_rowT(t):
                dve.wait_ge(s["h2T_psum"], t + 1)
                if t >= 1:
                    dve.wait_ge(s["lg_psum"], t)
                for f in range(2):
                    i = dve.tensor_tensor(H2T[:, 4 * f:4 * f + 4, :], PS[:, 4 + f, :].rearrange("p (k c) -> p k c", k=4),
                                          bc(prm_c("n2g", 4 * f, 4), P), ALU.mult)
                i.then_inc(s["h2T_ready"], 1)

            for t in range(NT):
                residual2(2 * t)
                if t >= 1:
                    router_rowT(t - 1)
                residual2(2 * t + 1)
                router_row(t)
            router_rowT(NT - 1)
            dve.wait_ge(s["lg_psum"], NT)
            lg = PS[:, 7, 0:NT * E].rearrange("p (t e) -> p t e", t=NT)
            own(dve.tensor_reduce(A4, lg, AX.X, ALU.max))
            own.settle()
            dve.tensor_tensor(AEX, lg, bc(A4, E), ALU.subtract).then_inc(s["lg_sub"], 1)
            dve.wait_ge(s["lg_exp"], 1)
            own(dve.tensor_reduce(A4B, AEX, AX.X, ALU.add))
            own.settle()
            own(dve.reciprocal(A4B, A4B))
            own.settle()
            dve.tensor_tensor(AFF, AEX, bc(A4B, E), ALU.mult).then_inc(s["aff_ready"], 1)
            dve.wait_ge(s["affT_psum"], 1)
            wk = AFFT[0:E, :]
            own(dve.tensor_copy(wk, PS[0:E, 1, :]))
            own.settle()
            for r in range(CAP // 8):
                v8 = VAL[0:E, 8 * r:8 * r + 8]
                own(dve.max(v8, wk))
                own.settle()
                own(dve.max_index(IDU[0:E, 8 * r:8 * r + 8], v8, wk))
                if r < CAP // 8 - 1:
                    own(dve.match_replace(wk, v8, wk, -1.0))
                own.settle()
            for f in range(2):
                own(dve.tensor_copy(IDF[0:E, f * CAP:(f + 1) * CAP], IDU[0:E, :]))
            dve.tensor_copy(VAL[0:E, CAP:2 * CAP], VAL[0:E, 0:CAP]).then_inc(s["tk_ready"], 1)
            dve.wait_ge(s["tkT_psum"], 1)
            dve.wait_ge(s["tab_in"], 112)
            own(dve.tensor_copy(IDXB[:, 0:CAP], PS[:, 2, CAP:2 * CAP]))

            def select(e):
                col = bass.ds(e * CAP, CAP)
                for t in range(NT):
                    i = dve.tensor_scalar(SEL[:, t, :], IDXB[:, col], iota_tok[:, t:t + 1], None, ALU.is_equal)
                i.then_inc(s["sel_ready"], 1)

            def gather_out(e):
                dve.wait_ge(s["gx_psum"], e + 1)
                dve.tensor_tensor(XE, PS[:, 7, :].rearrange("p (k c) -> p k c", k=KD), bc(prm_c("n2g", 0, 8), CAP), ALU.mult).then_inc(s["xe_ready"], 1)

            def expert(e, select_more, last_one):
                dve.wait_ge(s["s1_done"], e + 1)
                dve.wait_ge(s["w13_used"], (e + 1) * (2 * KD))
                dve.tensor_tensor(HH, S1, PF[:, 3 * 512:3 * 512 + FH], ALU.mult).then_inc(s["hh_done"], 1)
                dve.tensor_scalar(G, iota_row, IDT[:, bass.ds(e, 1)], GT[:, bass.ds(e, 1)], ALU.is_equal, ALU.mult).then_inc(s["gates_ready"], 1)
                if not last_one:
                    gather_out(e + 1)
                dve.wait_ge(s["ht_psum"], e + 1)
                dve.tensor_copy(HT[:, 4:FJ, :], PF[:, 4 * P:FH].rearrange("p (j c) -> p j c", c=P)).then_inc(s["ht_evD"], 1)
                if select_more:
                    dve.wait_ge(s["xe_ready"], e + 2)
                    select(e + 2)
                dve.wait_ge(s["w2_used"], (e + 1) * (2 * N2))
                dve.tensor_copy(YE, PS[:, 6, :]).then_inc(s["ye_ready"], 1)
                for n in range(2 * NT):
                    t, d = n // 2, n % 2
                    dve.wait_ge(s["sc_psum"], e * (2 * NT) + n + 1)
                    xs = X[:, t, d * 512:(d + 1) * 512]
                    dve.tensor_tensor(xs, xs, PS[:, [3, 4, 5, 7][n % 4], :], ALU.add).then_inc(s["sc_add"], 1)

            own.settle()
            select(0)
            own(dve.tensor_copy(IDT, PS[:, 2, 0:E]))
            own(dve.tensor_copy(GT, PS[:, 2, E:2 * E]))
            idd = IDD[0:E, :].rearrange("p (e c) -> p e c", e=E)
            dve.tensor_tensor(idd, bc(ident[0:E, 0:E], CAP), IDF[0:E, 0:CAP].unsqueeze(1).to_broadcast([E, E, CAP]), ALU.mult).then_inc(s["idd_ready"], 1)
            gather_out(0)
            dve.wait_ge(s["tkT_psum"], 2)
            own(dve.tensor_copy(IDXB, PF[:, 3 * 512:5 * 512]))
            own.settle()
            select(1)
            with dve.Fori(0, E - 2) as e:
                expert(e, True, False)
            expert(E - 2, False, False)
            expert(E - 1, False, True)

        @block.tensor
        def _(pe):
            def project(dst, lhs, rhs, inc=None, v=None):
                for k in range(KD):
                    i = pe.matmul(dst, lhs(k), rhs(k), start=k == 0, stop=k == KD - 1)
                if inc:
                    i.then_inc(s[inc], 1)
                return i

            pe.wait_ge(s["cst_in"], 32)
            for t in range(5):
                _, n = toks(t)
                pe.wait_ge(s["u_ready"], t + 1)
                if t >= 2:
                    pe.wait_ge(s["ut_ready"], t - 1)
                for k in range(KD):
                    i = pe.transpose(PS[:, 2 * (t % 2) + k // 4, (k % 4) * P:(k % 4) * P + n], U[t % 2][0:n, k * P:(k + 1) * P], ident[0:n, 0:n])
                i.then_inc(s["ut_psum"], 1)
            pe.wait_ge(s["ut_ready"], 5)
            pe.wait_ge(ws_in[0], ws_level[0])
            w = group(0)
            for b in range(3):
                project(PS[:, 4 + b, :], lambda k: w[:, k, b * P:(b + 1) * P], lambda k: UT[:, k, 0:S], "lat_psum")
            project(PS[:, 7, 0:META], lambda k: w[:, k, 2 * P:3 * P], lambda k: UT[:, k, S:LT], "lat_psum")
            pe.wait_ge(ws_in[1], ws_level[1])
            w1g = group(1)
            for t in range(5):
                c, n = toks(t)
                i = project(PS[0:n, 2, 32 * t:32 * t + 32], lambda k: UT[:, k, c:c + n], lambda k: w1g[:, k, 0:32])
            i.then_inc(s["kr_psum"], 1)
            pe.wait_ge(s["sq_ready"], 4)
            pe.wait_ge(s["lat_ready"], 4)
            pe.wait_ge(s["gp_init"], 1)
            for t in range(NT):
                for b in range(2):
                    pe.matmul(PS[:, 7, 32 + t:33 + t], SQ[:, b * 512 + t * P:b * 512 + (t + 1) * P], ones, start=b == 0, stop=b == 1)
            for t in range(5):
                c, n = toks(t)
                i = pe.matmul(PS[0:n, 7, 36 + t:37 + t], SQ[:, 1024 + c:1024 + c + n], ones, start=True, stop=True)
            i.then_inc(s["stat_psum"], 1)
            for t in range(NT):
                if t >= 2:
                    pe.wait_ge(s["mz_free"], t - 1)
                project(PS[:, t % 2, :], lambda k: w1g[:, k, 32 + t * P:32 + (t + 1) * P], lambda k: UT[:, k, 0:S], "mz_psum")
            pe.wait_ge(s["tab_in"], 112)

            def up(t):
                c, n = toks(t)
                if t >= 1:
                    pe.wait_ge(s["qk_evac"], t)
                if t < NT:
                    for f in range(2):
                        for b in range(2):
                            pe.matmul(PS[:, 3 + f, 0:384], CQT[:, b * S + c:b * S + c + P], UPW[:, b * 768 + f * 384:b * 768 + (f + 1) * 384],
                                      start=b == 0, stop=b == 1)
                for f in range(2):
                    i = pe.matmul(PS[0:n, 5 + f, :], CKVT[:, c:c + n], UPW[:, 1536 + f * 512:1536 + (f + 1) * 512], start=True, stop=True)
                i.then_inc(s["qk_psum"], 1)

            def turn_q(t):
                pe.wait_ge(s["q_ready"], t + 1)
                pe.wait_ge(s["rrT_evac"], t) if t >= 1 else pe.wait_ge(s["mz_free"], 4)
                for h in range(MH):
                    i = pe.transpose(PS[0:QH, h // 4, (h % 4) * P:(h % 4 + 1) * P], QTOK[t % 2][:, h * QH:(h + 1) * QH], ident)
                i.then_inc(s["qT_psum"], 1)

            def turn_k(t):
                c, n = toks(t)
                pe.wait_ge(s["k_ready"], t + 1)
                pe.wait_ge(s["qT_evac"], t + 1) if t < NT else pe.wait_ge(s["rrT_evac"], NT)
                for h in range(MH):
                    i = pe.transpose(PS[0:QH, h // 4, (h % 4) * P:(h % 4) * P + n], KTOK[t % 2][0:n, h * QH:(h + 1) * QH], ident[0:n, 0:n])
                i.then_inc(s["kT_psum"], 1)

            def ret_in(i):
                t = i % 5
                c, n = toks(t)
                g = 2 + (i >= 5)
                if i in (0, 5):
                    pe.wait_ge(ws_in[g % 2], ws_level[g])
                if i == 0:
                    pe.wait_ge(s["kr_copied"], 1)
                elif i == 1:
                    pe.wait_ge(s["lat_rstd"], 1)
                elif i < 7:
                    pe.wait_ge(s["e_free"], i - 1)
                else:
                    pe.wait_ge(s["rv_evac"], i - 6)
                wg = group(g)
                b = [2, 7][i % 2]
                if i >= 10:
                    j = i - 10
                    project(PS[:, b, :], lambda k: wg[:, k, 256 + j * P:256 + (j + 1) * P], lambda k: UT[:, k, 0:S], "e_psum")
                elif i >= 5:
                    project(PS[0:n, b, 0:256], lambda k: UT[:, k, c:c + n], lambda k: wg[:, k, 0:256], "e_psum")
                elif t < NT:
                    project(PS[:, b, :], lambda k: UT[:, k, c:c + n], lambda k: wg[:, k, :], "e_psum")
                else:
                    project(PS[0:n, b, 256:512], lambda k: UT[:, k, c:c + n], lambda k: wg[:, k, 256:512], "e_psum")

            def turn_ret(t):
                c, n = toks(t)
                pe.wait_ge(s["rr_ready"], t + 1)
                pe.wait_ge(s["kT_evac"], t + 1)
                for j in range(0 if t < NT else 2, 4):
                    i = pe.transpose(PS[:, 0, j * P:j * P + n], RT1[0:n, j * P:(j + 1) * P], ident[0:n, 0:n])
                i.then_inc(s["rrT_psum"], 1)

            up(0), up(1), ret_in(0), turn_q(0), up(2), turn_k(0), ret_in(1), turn_ret(0), turn_q(1), up(3), turn_k(1)
            ret_in(2), turn_ret(1), turn_q(2), up(4), turn_k(2), ret_in(3), turn_ret(2), turn_q(3), ret_in(4), turn_k(3)
            turn_ret(3), ret_in(5), turn_k(4), ret_in(6), turn_ret(4)
            for i in range(7, 12):
                ret_in(i)
            def ret_scores(h):
                j, o = h // 2, 64 * (h % 2)
                for b in range(5):
                    i = 5 * h + b
                    if i >= 4:
                        pe.wait_ge(s["ret_s"], i - 3)
                    c, n = toks(b)
                    q0 = c if b < NT else 0
                    pe.matmul(PS[0:n, i % 4, 0:S - q0], RKT[o:o + 64, j, c:c + n], RQT[o:o + 64, j, q0:S], start=True, stop=True)\
                        .then_inc(s["rs_psum"], 1)

            def ret_out(j):
                pe.wait_ge(s["ret_s"], 10 * j + 10)
                for b in range(5):
                    for f in range(2):
                        h = 2 * j + f
                        if b < NT:
                            i = pe.matmul(PS[64 * f:64 * f + 64, 6 + j, b * P:S], RV[:, b * 256 + h * 64:b * 256 + h * 64 + 64],
                                          SD[h][:, [0, 512, 896, 1152][b]:][:, 0:S - b * P], start=b == 0, stop=False, skip_group_check=True)
                        else:
                            i = pe.matmul(PS[64 * f:64 * f + 64, 6 + j, :], RV[0:META, 1024 + h * 64:1088 + h * 64], SD[h][0:META, 1280:1792],
                                          start=False, stop=True, skip_group_check=True)
                i.then_inc(s["ro_psum"], 1)

            def ret_mean(j):
                pe.wait_ge(s["ro_sq"], j + 1)
                pe.matmul(PS[:, 4 + j, :], ret_ones, RSQ[j], start=True, stop=True).then_inc(s["ro_ms"], 1)

            pe.wait_ge(s["qk_evac"], 5)
            pe.wait_ge(s["rrT_evac"], 5)
            pe.wait_ge(s["kT_evac"], 5)
            pe.wait_ge(s["rv_evac"], 5)
            pe.wait_ge(s["e_free"], 6)
            ret_scores(0)
            pe.wait_ge(s["e_free"], 7)
            ret_scores(1), ret_scores(2), ret_out(0), ret_scores(3), ret_mean(0), ret_out(1)
            pe.wait_ge(s["ret_s"], 5 * RH)
            for n in range(8):
                g = 4 + n // 4
                if n % 4 == 0:
                    pe.wait_ge(ws_in[g % 2], ws_level[g])
                if n >= 4:
                    pe.wait_ge(s["cc_evac"] if n % 2 == 0 else s["cx_done"], (n - 4) // 2 + 1)
                if n in (1, 2):
                    pe.wait_ge(s["ro_v"], n)
                if n == 3:
                    pe.wait_ge(s["yr_ready"], 2)
                wg = group(g)
                blk = (n % 2) * 256 + ((n % 4) // 2) * P
                if n < 4:
                    project(PS[:, [0, 1, 2, 7][n], 0:2], lambda k: wg[:, k, blk:blk + P], lambda k: UT[:, k, LT - 2:LT])
                project(PS[:, 3 + n % 4, :], lambda k: wg[:, k, blk:blk + P], lambda k: UT[:, k, 0:S], "f_psum")
                if n == 0:
                    ret_mean(1)

            def scores(i):
                t, h, b = i // MH, i % MH, score_bank(i)
                n = (t + 1) * P + META
                if i >= (NT - 1) * MH:
                    pe.wait_ge(s["p_done"], i - 1 if i > (NT - 1) * MH else i - 2)
                elif i >= 4:
                    pe.wait_ge(s["p_done"], i - 3)
                q = QT[0:QH + NT, h, t * P:(t + 1) * P]
                m = min(n, 512)
                ins = pe.matmul(PS[:, b, 0:m], q, KT[0:QH + NT, h, 0:m], start=True, stop=True)
                if n > m:
                    ins = pe.matmul(PS[:, b + 1, 0:n - m], q, KT[0:QH + NT, h, m:n], start=True, stop=True)
                ins.then_inc(s["s_psum"], 1)

            def turn_p(n):
                t = n // 4
                pe.wait_ge(s["ps_ready"], n + 1)
                if n >= 1:
                    pe.wait_ge(s["pt_evac"], n)
                    pe.wait_ge(s["ptm_evac"], n)
                for f in range(2):
                    p = PB[(2 * n + f) % 6]
                    for b in range(t + 1):
                        pe.transpose(PS[:, 4 + f, b * P:(b + 1) * P], p[:, META + b * P:META + (b + 1) * P], ident)
                    i = pe.transpose(PS[0:META, 6, f * P:(f + 1) * P], p[:, 0:META], ident)
                i.then_inc(s["pt_psum"], 1)

            def values(n):
                t, j = n // 4, n % 4
                pe.wait_ge(s["pt_evac"], n + 1)
                pe.wait_ge(s["ptm_evac"], n + 1)
                if j == 0 and t >= 1:
                    pe.wait_ge(s["yo_free"], t)
                for b in range(t + 2):
                    for f in range(2):
                        h = 2 * j + f
                        dst = PS[64 * f:64 * f + 64, 7, j * P:(j + 1) * P]
                        if b <= t:
                            i = pe.matmul(dst, V1[:, b * 512 + h * VH:b * 512 + (h + 1) * VH], PT[:, f, b * P:(b + 1) * P],
                                          start=b == 0, stop=False, skip_group_check=True)
                        else:
                            i = pe.matmul(dst, V1[0:META, NT * 512 + h * VH:NT * 512 + (h + 1) * VH], PTM[0:META, f, :],
                                          start=False, stop=True, skip_group_check=True)
                i.then_inc(s["pv_psum"], 1)

            pe.wait_ge(s["cz_done"], 1)
            pe.wait_ge(s["cx_done"], 2)
            for i in range(4):
                scores(i)
            pe.wait_ge(s["cz_done"], 2)
            for n in range(NT * 4):
                ahead = n + 2 if n + 2 < (NT - 1) * 4 else n + 1
                if ahead == n + 2 or (NT - 1) * 4 <= ahead < NT * 4:
                    scores(2 * ahead), scores(2 * ahead + 1)
                if n >= 1:
                    values(n - 1)
                turn_p(n)
            values(NT * 4 - 1)

            pe.wait_ge(s["yo_free"], NT)
            pe.wait_ge(s["yr_ready"], 2)
            pe.wait_ge(s["conv_y"], 2)
            def out_project(i):
                t, n = i // 2, i % 2
                if t == 0:
                    pe.wait_ge(ws_in[(6 + n) % 2], ws_level[6 + n])
                if i >= 4:
                    pe.wait_ge(s["xo_done"], i - 3)
                wg = group(6 + n)
                project(PS[:, i % 4, :], lambda k: YT[:, k, t * P:(t + 1) * P] if k < 6 else SRZ[:, (k - 6) * 512 + t * P:(k - 6) * 512 + (t + 1) * P],
                        lambda k: wg[:, k, :], "op_psum")

            def turn_row(t):
                pe.wait_ge(s["u2_ready"], t + 1)
                if t >= 2:
                    pe.wait_ge(s["ut2_ready"], t - 1)
                for k in range(KD):
                    i = pe.transpose(PS[:, 4 + 2 * (t % 2) + k // 4, (k % 4) * P:(k % 4 + 1) * P], U2[t % 2][:, k * P:(k + 1) * P], ident)
                i.then_inc(s["ut2_psum"], 1)

            for t in range(NT):
                out_project(2 * t)
                if t >= 1:
                    turn_row(t - 1)
                out_project(2 * t + 1)
            turn_row(NT - 1)
            pe.wait_ge(s["ut2_ready"], NT)
            pe.wait_ge(s["xo_done"], 2 * NT)
            for j in range(4):
                g = 8 + j // 2
                if j % 2 == 0:
                    pe.wait_ge(ws_in[g % 2], ws_level[g])
                if j >= 2:
                    pe.wait_ge(s["cu_done"], j - 1)
                wg = group(g)
                for f in range(2):
                    blk = f * 256 + (j % 2) * P
                    project(PS[:, (2 * j + f) % 4, :], lambda k: wg[:, k, blk:blk + P], lambda k: UT2[:, k, :], "f2_psum")

            def turn_z(i):
                pe.wait_ge(s["zr_ready"], i + 1)
                if i >= 2:
                    pe.wait_ge(s["zT_evac"], i - 1)
                else:
                    pe.wait_ge(s["cu_done"], 4)
                for j in range(4):
                    ins = pe.transpose(PS[:, i % 2, j * P:(j + 1) * P], XT1[:, j * P:(j + 1) * P], ident)
                ins.then_inc(s["zT_psum"], 1)

            for i in range(3 * NT):
                g, t = 10 + i // NT, i % NT
                if t == 0:
                    pe.wait_ge(ws_in[g % 2], ws_level[g])
                if i >= 4:
                    pe.wait_ge(s["z_free"], i - 3)
                wg = group(g)
                project(PS[:, 4 + i % 4, :], lambda k: UT2[:, k, t * P:(t + 1) * P], lambda k: wg[:, k, :], "z_psum")
                if 1 <= i <= 2 * NT:
                    turn_z(i - 1)

            def scores2(n):
                t, j = n // 4, n % 4
                if n >= 2:
                    pe.wait_ge(s["nm2_ready"], 2 * n - 2)
                for f in range(2):
                    pe.matmul(PS[:, 2 * (n % 2) + f, :], QT2[64 * f:64 * f + 64, j, t * P:(t + 1) * P], KT2[64 * f:64 * f + 64, j, :],
                              start=True, stop=True).then_inc(s["s2_psum"], 1)

            def turn_p2(n):
                pe.wait_ge(s["ps2_ready"], n + 1)
                if n >= 1:
                    pe.wait_ge(s["pt2_evA"], n)
                for f in range(2):
                    for b in range(NT):
                        ins = pe.transpose(PS[:, 4 + f, b * P:(b + 1) * P], SM[(2 * n + f) % 6][:, b * P:(b + 1) * P], ident)
                ins.then_inc(s["pt2_psum"], 1)

            def values2(n):
                t, j = n // 4, n % 4
                pe.wait_ge(s["pt2_evA"], n + 1)
                if j == 0 and t >= 1:
                    pe.wait_ge(s["yt2_evac"], t)
                for b in range(NT):
                    for f in range(2):
                        h = 2 * j + f
                        ins = pe.matmul(PS[64 * f:64 * f + 64, 6, j * P:(j + 1) * P], V2[:, b * 512 + h * HD:b * 512 + (h + 1) * HD],
                                        PT2[:, f, b * P:(b + 1) * P], start=b == 0, stop=b == NT - 1, skip_group_check=True)
                ins.then_inc(s["pv2_psum"], 1)

            pe.wait_ge(s["zT_evac"], 2 * NT)
            pe.wait_ge(s["v_evac"], NT)
            scores2(0), scores2(1)
            for n in range(NT * 4):
                if n + 2 < NT * 4:
                    scores2(n + 2)
                if n >= 1:
                    values2(n - 1)
                turn_p2(n)
                if n == LN_AT:
                    pe.wait_ge(s["cv_done"], 2)
                    pe.wait_ge(s["tap_added"], 2 * TAPS - 2)
                    for j in range(4):
                        ins = pe.matmul(PS[:, 7, :], LN_ONES, CA[:, j, :], start=j == 0, stop=j == 3)
                    ins.then_inc(s["mean_psum"], 1)
                if n == LN_AT + 2:
                    pe.wait_ge(s["cen_done"], 4)
                    pe.wait_ge(s["lsq_done"], 4)
                    for j in range(4):
                        ins = pe.matmul(PS[:, 7, :], LN_ONES, LSQ[:, j, :], start=j == 0, stop=j == 3)
                    ins.then_inc(s["var_psum"], 1)
            values2(NT * 4 - 1)
            pe.wait_ge(s["yt2_evac"], NT)
            pe.wait_ge(s["y2_done"], 4)
            pe.wait_ge(s["lrs_done"], 1)
            pe.wait_ge(s["lv_ready"], 1)
            pe.wait_ge(s["tab_in"], 112)

            def out_project2(i):
                t, n = i // 2, i % 2
                if t == 0:
                    pe.wait_ge(ws_in[(13 + n) % 2], ws_level[13 + n])
                if i >= 4:
                    pe.wait_ge(s["xo2_done"], i - 3)
                wg = group(13 + n)
                project(PS[:, i % 4, :], lambda k: YT2[:, k, t * P:(t + 1) * P], lambda k: wg[:, k, :], "op2_psum")

            def router_turn(t):
                pe.wait_ge(s["h2_ready"], t + 1)
                if t >= 1:
                    pe.wait_ge(s["h2T_ready"], t)
                for k in range(KD):
                    i = pe.transpose(PS[:, 4 + k // 4, (k % 4) * P:(k % 4 + 1) * P], HR[t % 2][:, k * P:(k + 1) * P], ident)
                i.then_inc(s["h2T_psum"], 1)

            def logits(t):
                pe.wait_ge(s["h2T_ready"], t + 1)
                for k in range(KD):
                    i = pe.matmul(PS[:, 7, t * E:(t + 1) * E], H2T[:, k, :], wr[:, k, :], start=k == 0, stop=k == KD - 1)
                i.then_inc(s["lg_psum"], 1)

            for t in range(NT):
                out_project2(2 * t)
                if t >= 1:
                    router_turn(t - 1)
                out_project2(2 * t + 1)
                if t >= 1:
                    logits(t - 1)
            router_turn(NT - 1)
            logits(NT - 1)
            pe.wait_ge(s["aff_ready"], 1)
            for t in range(NT):
                i = pe.transpose(PS[0:E, 1, t * P:(t + 1) * P], AFF[:, t, :], ident)
            i.then_inc(s["affT_psum"], 1)
            pe.wait_ge(s["tk_ready"], 1)
            pe.transpose(PS[:, 2, 0:E], IDF[0:E, :], ident[0:E, 0:E])
            pe.transpose(PS[:, 2, E:2 * E], VAL[0:E, :], ident[0:E, 0:E])
            pe.matmul(PS[:, 2, CAP:2 * CAP], ident[0:E, 0:1].to_broadcast([E, P]), IDF[0:E, 0:CAP], start=True, stop=True).then_inc(s["tkT_psum"], 1)

            def gather(e):
                pe.wait_ge(s["sel_ready"], e + 1)
                for k in range(KD):
                    for t in range(NT):
                        i = pe.matmul(PS[:, 7, k * CAP:(k + 1) * CAP], H2N[:, t, k * P:(k + 1) * P], SEL[:, t, :], start=t == 0, stop=t == NT - 1)
                i.then_inc(s["gx_psum"], 1)

            def up13(e, third):
                bank = 3 if third else 0
                for k in range(KD):
                    pe.wait_ge(w13_in[k], (2 * e + (2 if third else 1)) * 16)
                    for c, n in FCH:
                        for f in range(2):
                            i = pe.matmul(PS[64 * f:64 * f + 64, bank + c // 512, 0:n], XE[:, k, :], W13[k][:, f * FH + c:f * FH + c + n],
                                          start=k == 0, stop=k == KD - 1, skip_group_check=True)
                    i.then_inc(s["w13_used"], 1)

            def expert(e, first, last_one):
                pe.wait_ge(s["xe_ready"], e + 1)
                if not first:
                    pe.wait_ge(s["ht_evD"], e)
                    pe.wait_ge(s["ht_evA"], e)
                up13(e, False)
                if first:
                    pe.wait_ge(s["sel_ready"], 2)
                else:
                    pe.wait_ge(s["sc_add"], e * (2 * NT))
                up13(e, True)
                if not last_one:
                    gather(e + 1)
                pe.wait_ge(s["hh_done"], e + 1)
                for j in range(FJ):
                    i = pe.transpose(PF[:, j * P:(j + 1) * P], HH[:, j * P:(j + 1) * P], ident)
                i.then_inc(s["ht_psum"], 1)
                pe.wait_ge(s["ht_evA"], e + 1)
                pe.wait_ge(s["ht_evD"], e + 1)
                for i in range(2 * FJ):
                    j, f = i // 2, i % 2
                    pe.wait_ge(w2_in[i % N2], (2 * e + i // N2 + 1) * 16)
                    for d in range(2):
                        ins = pe.matmul(PS[64 * d:64 * d + 64, 6, :], HT[:, j, 64 * f:64 * f + 64], W2S[i % N2][:, d * 512:(d + 1) * 512],
                                        start=i == 0, stop=i == 2 * FJ - 1, skip_group_check=True)
                    ins.then_inc(s["w2_used"], 1)
                pe.wait_ge(s["ye_ready"], e + 1)
                pe.wait_ge(s["gates_ready"], e + 1)
                if not last_one:
                    pe.wait_ge(s["xe_ready"], e + 2)
                for n in range(2 * NT):
                    t, d = n // 2, n % 2
                    if n >= 4:
                        pe.wait_ge(s["sc_add"], e * (2 * NT) + n - 3)
                    pe.matmul(PS[:, [3, 4, 5, 7][n % 4], :], G[64 * d:64 * d + 64, t * P:(t + 1) * P], YE[64 * d:64 * d + 64, :],
                              start=True, stop=True).then_inc(s["sc_psum"], 1)

            pe.wait_ge(s["h2n_ready"], NT)
            gather(0)
            pe.wait_ge(s["idd_ready"], 1)
            for f in range(2):
                i = pe.matmul(PS[:, 3 + f, :], ones[0:E, :].to_broadcast([E, P]), IDD[0:E, f * 512:(f + 1) * 512], start=True, stop=True)
            i.then_inc(s["tkT_psum"], 1)
            expert(0, True, False)
            with pe.Fori(1, E - 1) as e:
                expert(e, False, False)
            expert(E - 1, False, True)


LN_AT = 8
TAPS_PER_TILE = 4
PRODUCTS_PER_TILE = 7


def _tables():
    f = np.float32

    def ropes(dim, pos):
        inv = (f(1.0) / (f(10000.0) ** (np.arange(0, dim, 2, dtype=f) / f(dim)))).astype(f)
        ang = (pos.astype(f)[..., None] * inv).astype(np.float64)
        c, sn = np.cos(ang), np.sin(ang)
        return np.concatenate([c, c], -1), np.concatenate([-sn, sn], -1)

    p = np.arange(P)
    pos1 = np.stack([META + t * P + p for t in range(NT)] + [p], 1)
    pos2 = np.stack([t * P + p for t in range(NT)], 1)
    tab = np.zeros((P, NTAB), f)

    def put(name, v):
        a, n = TAB[name]
        tab[:, a:a + n] = v.reshape(P, n)

    for names, dim, pos in ((("mcc", "mss"), ROPE, pos1), (("rcc", "rss"), RD, pos1), (("bcc", "bss"), HD, pos2)):
        for name, v in zip(names, ropes(dim, pos)):
            put(name, v)
    c = np.arange(LT)
    lg = np.log1p(-np.exp2(-5.0 - np.arange(RH)))
    d = np.exp(lg[None, :, None] * np.abs(c[None, None, :] - p[:, None, None])) * RD ** -0.5
    put("dec", np.where((p[:, None] // 64 <= c[None, :] // 64)[:, None, :], d, 0.0))
    put("rones", np.where(p[:, None] // 64 == p[None, :] // 64, 1.0 / RD, 0.0))
    y = np.arange(2 * S - P)
    dist = np.abs(p[:, None] - (y[None, :] - (S - P)))
    n = (dist <= 64) * 1 + ((dist % 4 == 0) & (dist <= 256)) + ((dist % 16 == 0) & (dist <= 1024))
    put("cm", np.where(n > 0, np.log(np.maximum(n, 1)), NEG))
    iota = np.concatenate([np.broadcast_to(np.arange(S, dtype=f), (P, S)), pos2.astype(f)], 1)
    b, c = np.arange(NT)[:, None], np.arange(S)[None, :]
    mask = np.zeros((NT, S + LT), f)
    mask[:, 0:S] = (c // P == b) & (c % P < 64)
    mask[:, S + META:] = np.where((c // P == b) & (c % P >= 64), NEG, 0.0)
    return tab, iota, mask


def kernel(**inputs):
    import concourse.bacc as bacc
    from concourse.bass_utils import run_bass_kernel_spmd

    v = {k: np.asarray(a) for k, a in inputs.items()}
    f = np.float32
    prm = np.ones((P, NPRM), f)

    def put(name, a):
        at, n = PRM[name]
        prm[:a.shape[0], at:at + n] = a.reshape(a.shape[0], n)

    def cols(a):
        return a.reshape(-1, P).T

    def rep(a):
        return np.broadcast_to(a, (P, a.shape[0]))

    def swap(a):
        h = a.shape[0] // 2
        return np.concatenate([a[h:], a[:h]])

    put("lnw", cols(v["ln_w"][0]))
    put("qan", cols(v["q_a_norm"][0]))
    put("kvan", cols(v["kv_a_norm"][0]))
    put("qn", v["q_norm"][0][:NOPE, None])
    put("kn", v["k_norm"][0][:NOPE, None])
    put("cw", v["conv_w"][0].reshape(3, 2, P).transpose(2, 1, 0))
    put("cb", cols(v["conv_b"][0]))
    put("n1g", cols(v["norm1_g_2"]))
    put("dw", v["conv_dw_w_2"].reshape(TAPS, 4, P).transpose(2, 1, 0))
    put("dwb", cols(v["conv_dw_b_2"]))
    put("lng", cols(v["conv_ln_g_2"]))
    put("lnb", cols(v["conv_ln_b_2"]))
    put("n2g", cols(v["norm2_g_2"]))
    for a, b, w in (("qr", "qrs", v["q_norm"][0][NOPE:]), ("kr", "krs", v["k_norm"][0][NOPE:]),
                    ("q2", "q2s", v["q_norm_g_2"]), ("k2", "k2s", v["k_norm_g_2"])):
        put(a, rep(w))
        put(b, rep(swap(w)))
    put("retc", np.concatenate([v["ret_norm"][0]] * 2)[:, None])
    tab, iota, mask = _tables()
    arrays = {
        "x": v["x"][0], "meta": v["meta_tokens"], "w_in": v["w_in"][0], "w_out": v["w_out"][0], "w_in_2": v["w_in_2"],
        "w_out_2": v["w_out_2"], "w_uq": v["w_uq"][0], "w_ukv": v["w_ukv"][0], "w_router": v["w_router_2"],
        "w1": v["w1_2"], "w3": v["w3_2"], "w2": v["w2_2"], "prm": prm, "ident": np.eye(P, dtype=f), "tab": tab, "iota": iota, "mask": mask,
    }
    arrays = {f"in_{k}": np.ascontiguousarray(a) for k, a in arrays.items()}
    nc = bacc.Bacc("TRN2", target_bir_lowering=False, num_devices=1)
    d = {k[3:]: nc.dram_tensor(k, a.shape, mybir.dt.from_np(a.dtype), kind="ExternalInput").ap() for k, a in arrays.items()}
    out = nc.dram_tensor("out_x", (S, D), F32, kind="ExternalOutput").ap()
    build(nc, d["x"], d["meta"], {k: d[k] for k in ("w_in", "w_out", "w_in_2", "w_out_2")}, d["w_uq"], d["w_ukv"], d["w_router"],
          d["w1"], d["w3"], d["w2"], d["prm"], d["ident"], d["tab"], d["iota"], d["mask"], out)
    r = run_bass_kernel_spmd(nc, [arrays], core_ids=[0])
    return r.results[0]["out_x"].reshape(1, S, D)
```
